# Optimizing a Trainium2 kernel written in Bass

```python
import math
import jax, jax.numpy as jnp
from jax import lax
import numpy as np

D_MODEL = 1024
BATCH = 1
SEQ = 256
DEPTH = 2

N_MEM = 256
A_HEADS = 4
A_QK_DIM = 64
A_V_DIM = 2 * A_QK_DIM
A_QK_COLS = A_HEADS * 2 * A_QK_DIM
A_WIDTH = A_HEADS * A_V_DIM
POOL_WINDOWS = (2, 4, 8, 16)
POOL_GROUPS = len(POOL_WINDOWS)
POOL_GROUP_DIM = (D_MODEL // 2) // POOL_GROUPS
POOL_WIDTH = POOL_GROUPS * POOL_GROUP_DIM
EVEN_IN = 2 * A_QK_COLS + A_WIDTH + POOL_WIDTH
EVEN_MIX = A_WIDTH + POOL_WIDTH
CONV_WIDTH = 3
CONV_DIM = D_MODEL
X_HEADS = 4
X_HEAD_DIM = D_MODEL // X_HEADS
D_FF = 4 * D_MODEL
REL_BUCKETS = 32
REL_MAX_EXACT = REL_BUCKETS // 2
REL_MAX_DIST = 128
Q_BLOCK = 128
N_EVEN = (DEPTH + 1) // 2
N_ODD = DEPTH // 2
EPS = 1e-6


def rms_norm(x, g):
    xf = x.astype(jnp.float32)
    y = xf * lax.rsqrt(jnp.mean(xf * xf, axis=-1, keepdims=True) + EPS)
    return (y * g.astype(jnp.float32)).astype(x.dtype)

def t5_bucket(n):
    small = n < REL_MAX_EXACT
    nf = jnp.maximum(n, 1).astype(jnp.float32)
    large = REL_MAX_EXACT + (jnp.log(nf / REL_MAX_EXACT)
                             / math.log(REL_MAX_DIST / REL_MAX_EXACT)
                             * (REL_BUCKETS - REL_MAX_EXACT)).astype(jnp.int32)
    large = jnp.minimum(large, REL_BUCKETS - 1)
    return jnp.where(small, n, large)

def diff_attention(q1, q2, k1, k2, v, lam, bias_dist):
    B, S = q1.shape[0], q1.shape[1]
    nb = S // Q_BLOCK
    scale = A_QK_DIM ** -0.5
    qb1 = q1.reshape(B, nb, Q_BLOCK, A_HEADS, A_QK_DIM).transpose(1, 0, 2, 3, 4)
    qb2 = q2.reshape(B, nb, Q_BLOCK, A_HEADS, A_QK_DIM).transpose(1, 0, 2, 3, 4)
    starts = jnp.arange(nb, dtype=jnp.int32) * Q_BLOCK
    kpos = jnp.arange(S, dtype=jnp.int32)

    def block(args):
        qa, qc, start = args
        qpos = start + jnp.arange(Q_BLOCK, dtype=jnp.int32)
        dist = qpos[:, None] - kpos[None, :]
        causal = dist >= 0
        bias = bias_dist[:, jnp.clip(dist, 0, S - 1)]

        def probs(q, k):
            s = jnp.einsum('bqhd,bkhd->bhqk', q, k).astype(jnp.float32) * scale + bias
            s = jnp.where(causal, s, -jnp.inf)
            return jax.nn.softmax(s, axis=-1)

        a = probs(qa, k1) - lam * probs(qc, k2)
        return jnp.einsum('bhqk,bkhd->bqhd', a.astype(v.dtype), v)

    out = lax.map(block, (qb1, qb2, starts))
    return out.transpose(1, 0, 2, 3, 4).reshape(B, S, A_HEADS, A_V_DIM)

def multi_scale_pool(u, pool_w, pool_scale):
    B, S = u.shape[0], u.shape[1]
    ug = u.reshape(B, S, POOL_GROUPS, POOL_GROUP_DIM).astype(jnp.float32)
    c = jnp.concatenate([jnp.zeros((B, 1, POOL_GROUPS, POOL_GROUP_DIM), jnp.float32),
                         jnp.cumsum(ug, axis=1)], axis=1)
    t = jnp.arange(S, dtype=jnp.int32)
    pooled = []
    for gi, w in enumerate(POOL_WINDOWS):
        cg = c[:, :, gi]
        cp = jnp.concatenate([jnp.zeros((B, w - 1, POOL_GROUP_DIM), jnp.float32), cg], axis=1)
        win_sum = cg[:, 1:] - cp[:, :S]
        count = jnp.minimum(t + 1, w).astype(jnp.float32)[None, :, None]
        pooled.append(win_sum / count - ug[:, :, gi])
    p = jnp.stack(pooled, axis=2).astype(u.dtype)
    y = jnp.einsum('bsgc,gcd->bsgd', p, pool_w) * pool_scale.reshape(POOL_GROUPS, POOL_GROUP_DIM)
    return y.reshape(B, S, POOL_WIDTH)

def even_mixer(h, w_in, w_out, lq1, lk1, lq2, lk2, subln_g, pool_w, pool_scale,
               bias_dist, lambda_init):
    B, S = h.shape[0], h.shape[1]
    proj = h @ w_in
    q = proj[..., :A_QK_COLS].reshape(B, S, A_HEADS, 2, A_QK_DIM)
    k = proj[..., A_QK_COLS:2 * A_QK_COLS].reshape(B, S, A_HEADS, 2, A_QK_DIM)
    v = proj[..., 2 * A_QK_COLS:2 * A_QK_COLS + A_WIDTH].reshape(B, S, A_HEADS, A_V_DIM)
    u = proj[..., 2 * A_QK_COLS + A_WIDTH:]
    lam = (jnp.exp(jnp.sum(lq1.astype(jnp.float32) * lk1.astype(jnp.float32)))
           - jnp.exp(jnp.sum(lq2.astype(jnp.float32) * lk2.astype(jnp.float32)))
           + lambda_init)
    o = diff_attention(q[..., 0, :], q[..., 1, :], k[..., 0, :], k[..., 1, :], v, lam, bias_dist)
    o = (rms_norm(o, subln_g) * (1.0 - lambda_init)).reshape(B, S, A_WIDTH)
    y = multi_scale_pool(u, pool_w, pool_scale)
    return jnp.concatenate([o, y], axis=-1) @ w_out

def odd_mixer(h, w_in, conv_w, w_out):
    S = h.shape[1]
    proj = h @ w_in
    b_gate = proj[..., :CONV_DIM]
    c_gate = proj[..., CONV_DIM:2 * CONV_DIM]
    z = c_gate * proj[..., 2 * CONV_DIM:]
    zp = jnp.pad(z, ((0, 0), (CONV_WIDTH - 1, 0), (0, 0)))
    y = zp[:, 0:S] * conv_w[0]
    for tap in range(1, CONV_WIDTH):
        y = y + zp[:, tap:tap + S] * conv_w[tap]
    return (b_gate * y) @ w_out

def cross_attention(h, mem_n, wq, wkv, wo):
    B, S = h.shape[0], h.shape[1]
    M = mem_n.shape[1]
    q = (h @ wq).reshape(B, S, X_HEADS, X_HEAD_DIM)
    kv = (mem_n @ wkv).reshape(B, M, 2, X_HEADS, X_HEAD_DIM)
    s = jnp.einsum('bshd,bmhd->bhsm', q, kv[:, :, 0]).astype(jnp.float32) * X_HEAD_DIM ** -0.5
    p = jax.nn.softmax(s, axis=-1)
    o = jnp.einsum('bhsm,bmhd->bshd', p.astype(h.dtype), kv[:, :, 1]).reshape(B, S, D_MODEL)
    return o @ wo

def sq_relu_mlp(h, w1, w2):
    a = jax.nn.relu(h @ w1)
    return (a * a) @ w2

def first_inputs(seed: int = 0) -> dict:
    key = jax.random.key(seed)
    ks = iter(jax.random.split(key, 32))
    f32 = jnp.float32

    def nrm(shape, scale):
        return jax.random.normal(next(ks), shape, f32) * scale

    def gain(shape):
        return 1.0 + nrm(shape, 0.02)

    return {
        "x": nrm((BATCH, SEQ, D_MODEL), 1.0),
        "mem": nrm((BATCH, N_MEM, D_MODEL), 1.0),
        "rel_bias": nrm((REL_BUCKETS, A_HEADS), 0.5),
        "mem_norm_g": gain((D_MODEL,)),
        "norm_mix_g": gain((DEPTH, D_MODEL)),
        "norm_xattn_g": gain((DEPTH, D_MODEL)),
        "norm_mlp_g": gain((DEPTH, D_MODEL)),
        "final_norm_g": gain((D_MODEL,)),
        "ab_w_in": nrm((N_EVEN, D_MODEL, EVEN_IN), D_MODEL ** -0.5),
        "ab_w_out": nrm((N_EVEN, EVEN_MIX, D_MODEL), EVEN_MIX ** -0.5),
        "lambda_q1": nrm((N_EVEN, A_QK_DIM), 0.1),
        "lambda_k1": nrm((N_EVEN, A_QK_DIM), 0.1),
        "lambda_q2": nrm((N_EVEN, A_QK_DIM), 0.1),
        "lambda_k2": nrm((N_EVEN, A_QK_DIM), 0.1),
        "subln_g": gain((N_EVEN, A_V_DIM)),
        "pool_w": nrm((N_EVEN, POOL_GROUPS, POOL_GROUP_DIM, POOL_GROUP_DIM), POOL_GROUP_DIM ** -0.5),
        "pool_scale": 1.0 + nrm((N_EVEN, POOL_WIDTH), 0.1),
        "conv_w_in": nrm((N_ODD, D_MODEL, 3 * CONV_DIM), D_MODEL ** -0.5),
        "conv_w": nrm((N_ODD, CONV_WIDTH, CONV_DIM), CONV_WIDTH ** -0.5),
        "conv_w_out": nrm((N_ODD, CONV_DIM, D_MODEL), CONV_DIM ** -0.5),
        "xattn_wq": nrm((DEPTH, D_MODEL, D_MODEL), D_MODEL ** -0.5),
        "xattn_wkv": nrm((DEPTH, D_MODEL, 2 * D_MODEL), D_MODEL ** -0.5),
        "xattn_wo": nrm((DEPTH, D_MODEL, D_MODEL), D_MODEL ** -0.5),
        "mlp_w1": nrm((DEPTH, D_MODEL, D_FF), D_MODEL ** -0.5),
        "mlp_w2": nrm((DEPTH, D_FF, D_MODEL), D_FF ** -0.5),
    }

def first_block(x, mem, rel_bias, mem_norm_g, norm_mix_g, norm_xattn_g, norm_mlp_g,
              final_norm_g, ab_w_in, ab_w_out, lambda_q1, lambda_k1, lambda_q2,
              lambda_k2, subln_g, pool_w, pool_scale, conv_w_in, conv_w, conv_w_out,
              xattn_wq, xattn_wkv, xattn_wo, mlp_w1, mlp_w2):
    S = x.shape[1]
    buckets = t5_bucket(jnp.arange(S, dtype=jnp.int32))
    bias_dist = rel_bias.astype(jnp.float32)[buckets].T
    mem_n = rms_norm(mem, mem_norm_g)
    h = x
    for l in range(DEPTH):
        i = l // 2
        hn = rms_norm(h, norm_mix_g[l])
        if l % 2 == 0:
            lambda_init = 0.8 - 0.6 * math.exp(-0.3 * l)
            h = h + even_mixer(hn, ab_w_in[i], ab_w_out[i], lambda_q1[i], lambda_k1[i],
                               lambda_q2[i], lambda_k2[i], subln_g[i], pool_w[i],
                               pool_scale[i], bias_dist, lambda_init)
        else:
            h = h + odd_mixer(hn, conv_w_in[i], conv_w[i], conv_w_out[i])
        h = h + cross_attention(rms_norm(h, norm_xattn_g[l]), mem_n,
                                xattn_wq[l], xattn_wkv[l], xattn_wo[l])
        h = h + sq_relu_mlp(rms_norm(h, norm_mlp_g[l]), mlp_w1[l], mlp_w2[l])
    return rms_norm(h, final_norm_g)


DEPTH_2 = 1

FOX_HEADS = 8
FOX_HEAD_DIM = 64
FOX_WIDTH = FOX_HEADS * FOX_HEAD_DIM
RET_HEADS = 4
RET_HEAD_DIM = 128
RET_WIDTH = RET_HEADS * RET_HEAD_DIM
MIX_WIDTH = FOX_WIDTH + RET_WIDTH
D_FF_2 = 4 * D_MODEL
RET_CHUNK = 128
ROPE_BASE = 10000.0
N_MOD = 6
IN_COLS = 4 * FOX_WIDTH + FOX_HEADS + 4 * RET_WIDTH


def _rms(x):
    x32 = x.astype(jnp.float32)
    return x32 * lax.rsqrt(jnp.mean(x32 * x32, axis=-1, keepdims=True) + EPS)

def _rope(x):
    s, d = x.shape[1], x.shape[-1]
    pos = jnp.arange(s, dtype=jnp.float32)
    inv_freq = ROPE_BASE ** (-jnp.arange(0, d, 2, dtype=jnp.float32) / d)
    ang = pos[:, None] * inv_freq[None, :]
    cos = jnp.cos(ang)[None, :, None, :]
    sin = jnp.sin(ang)[None, :, None, :]
    x32 = x.astype(jnp.float32)
    x1, x2 = x32[..., : d // 2], x32[..., d // 2:]
    return jnp.concatenate([x1 * cos - x2 * sin, x1 * sin + x2 * cos], axis=-1).astype(x.dtype)

def _forgetting_attention(q, k, v, log_f):
    b, s, h, d = q.shape
    scale = 1.0 / np.sqrt(d)
    cum = jnp.cumsum(log_f, axis=1).transpose(0, 2, 1)
    qh = q.transpose(0, 2, 1, 3)
    kh = k.transpose(0, 2, 1, 3)
    vh = v.transpose(0, 2, 1, 3)
    outs = []
    for blk in range(s // Q_BLOCK):
        s0, s1 = blk * Q_BLOCK, (blk + 1) * Q_BLOCK
        logits = jnp.einsum('bhqd,bhkd->bhqk', qh[:, :, s0:s1], kh[:, :, :s1]).astype(jnp.float32) * scale
        logits = logits + cum[:, :, s0:s1, None] - cum[:, :, None, :s1]
        q_pos = jnp.arange(s0, s1)[:, None]
        k_pos = jnp.arange(s1)[None, :]
        logits = jnp.where(q_pos >= k_pos, logits, -jnp.inf)
        p = jax.nn.softmax(logits, axis=-1).astype(v.dtype)
        outs.append(jnp.einsum('bhqk,bhkd->bhqd', p, vh[:, :, :s1]))
    out = jnp.concatenate(outs, axis=2)
    return out.transpose(0, 2, 1, 3)

def _retention(q, k, v):
    b, s, h, dk = q.shape
    dv = v.shape[-1]
    n_chunks = s // RET_CHUNK
    log_g = jnp.log(1.0 - 2.0 ** (-5.0 - jnp.arange(h, dtype=jnp.float32)))
    n = jnp.arange(RET_CHUNK, dtype=jnp.float32)
    diff = n[:, None] - n[None, :]
    decay_mask = jnp.where(diff[None] >= 0,
                           jnp.exp(jnp.maximum(diff, 0.0)[None] * log_g[:, None, None]), 0.0)
    xi = jnp.exp((n[None, :] + 1.0) * log_g[:, None])
    zeta = jnp.exp((RET_CHUNK - 1.0 - n[None, :]) * log_g[:, None])
    g_chunk = jnp.exp(RET_CHUNK * log_g)

    def to_chunks(t):
        return t.astype(jnp.float32).reshape(b, n_chunks, RET_CHUNK, h, t.shape[-1]).transpose(1, 0, 3, 2, 4)

    qc, kc, vc = to_chunks(q), to_chunks(k * (dk ** -0.5)), to_chunks(v)

    def step(state, inp):
        qi, ki, vi = inp
        inner = jnp.einsum('bhnd,bhmd->bhnm', qi, ki) * decay_mask[None]
        inner_out = jnp.einsum('bhnm,bhmv->bhnv', inner, vi)
        cross_out = jnp.einsum('bhnd,bhdv->bhnv', qi, state) * xi[None, :, :, None]
        new_state = state * g_chunk[None, :, None, None] + \
            jnp.einsum('bhmd,bhmv->bhdv', ki * zeta[None, :, :, None], vi)
        return new_state, inner_out + cross_out

    state0 = jnp.zeros((b, h, dk, dv), jnp.float32)
    _, out = lax.scan(step, state0, (qc, kc, vc))
    return out.transpose(1, 0, 3, 2, 4).reshape(b, s, h, dv)

def second_inputs(seed: int = 0) -> dict:
    key = jax.random.key(seed)
    ks = jax.random.split(key, 16)
    nrm = jax.random.normal
    f32 = jnp.float32
    return {
        "x": nrm(ks[0], (BATCH, SEQ, D_MODEL), f32),
        "c": nrm(ks[1], (BATCH, D_MODEL), f32),
        "w_ada": nrm(ks[2], (DEPTH_2, D_MODEL, N_MOD * D_MODEL), f32) * (0.5 * D_MODEL ** -0.5),
        "b_ada": nrm(ks[3], (DEPTH_2, N_MOD * D_MODEL), f32) * 0.02,
        "w_in": nrm(ks[4], (DEPTH_2, D_MODEL, IN_COLS), f32) * D_MODEL ** -0.5,
        "b_forget": 2.0 + 0.5 * nrm(ks[5], (DEPTH_2, FOX_HEADS), f32),
        "q_norm_gain": 1.0 + 0.05 * nrm(ks[6], (DEPTH_2, FOX_HEAD_DIM), f32),
        "k_norm_gain": 1.0 + 0.05 * nrm(ks[7], (DEPTH_2, FOX_HEAD_DIM), f32),
        "fox_out_gain": 1.0 + 0.05 * nrm(ks[8], (DEPTH_2, FOX_HEADS, FOX_HEAD_DIM), f32),
        "ret_out_gain": 1.0 + 0.05 * nrm(ks[9], (DEPTH_2, RET_HEADS, RET_HEAD_DIM), f32),
        "w_out": nrm(ks[10], (DEPTH_2, MIX_WIDTH, D_MODEL), f32) * MIX_WIDTH ** -0.5,
        "w_mlp_in": nrm(ks[11], (DEPTH_2, D_MODEL, D_FF_2), f32) * D_MODEL ** -0.5,
        "w_mlp_out": nrm(ks[12], (DEPTH_2, D_FF_2, D_MODEL), f32) * D_FF_2 ** -0.5,
    }

def second_block(x, c, w_ada, b_ada, w_in, b_forget, q_norm_gain, k_norm_gain,
              fox_out_gain, ret_out_gain, w_out, w_mlp_in, w_mlp_out):
    b, s, _ = x.shape
    dt = x.dtype
    c_act = jax.nn.silu(c)
    o_fq, o_fk, o_fv, o_fog = 0, FOX_WIDTH, 2 * FOX_WIDTH, 3 * FOX_WIDTH
    o_ff = 4 * FOX_WIDTH
    o_rq = o_ff + FOX_HEADS
    o_rk, o_rv, o_rg = o_rq + RET_WIDTH, o_rq + 2 * RET_WIDTH, o_rq + 3 * RET_WIDTH
    for l in range(DEPTH_2):
        mod = jnp.einsum('bd,de->be', c_act, w_ada[l]) + b_ada[l]
        shift_m, scale_m, gate_m, shift_f, scale_f, gate_f = [m[:, None, :] for m in jnp.split(mod, N_MOD, axis=-1)]

        h = (_rms(x) * (1.0 + scale_m) + shift_m).astype(dt)
        proj = jnp.einsum('bsd,de->bse', h, w_in[l])

        fq = proj[..., o_fq:o_fk].reshape(b, s, FOX_HEADS, FOX_HEAD_DIM)
        fk = proj[..., o_fk:o_fv].reshape(b, s, FOX_HEADS, FOX_HEAD_DIM)
        fv = proj[..., o_fv:o_fog].reshape(b, s, FOX_HEADS, FOX_HEAD_DIM)
        f_og = proj[..., o_fog:o_ff]
        f_logit = proj[..., o_ff:o_rq]
        fq = (_rms(fq) * q_norm_gain[l]).astype(dt)
        fk = (_rms(fk) * k_norm_gain[l]).astype(dt)
        log_f = jax.nn.log_sigmoid(f_logit.astype(jnp.float32) + b_forget[l])
        fox = _forgetting_attention(fq, fk, fv, log_f)
        fox = (_rms(fox) * fox_out_gain[l]).reshape(b, s, FOX_WIDTH) * jax.nn.sigmoid(f_og.astype(jnp.float32))

        rq = _rope(proj[..., o_rq:o_rk].reshape(b, s, RET_HEADS, RET_HEAD_DIM))
        rk = _rope(proj[..., o_rk:o_rv].reshape(b, s, RET_HEADS, RET_HEAD_DIM))
        rv = proj[..., o_rv:o_rg].reshape(b, s, RET_HEADS, RET_HEAD_DIM)
        r_gate = proj[..., o_rg:]
        ret = _retention(rq, rk, rv)
        ret = (_rms(ret) * ret_out_gain[l]).reshape(b, s, RET_WIDTH) * jax.nn.silu(r_gate.astype(jnp.float32))

        mixed = jnp.concatenate([fox, ret], axis=-1).astype(dt)
        x = x + gate_m * jnp.einsum('bse,ed->bsd', mixed, w_out[l])

        h = (_rms(x) * (1.0 + scale_f) + shift_f).astype(dt)
        u = jnp.square(jax.nn.relu(jnp.einsum('bsd,df->bsf', h, w_mlp_in[l])))
        x = x + gate_f * jnp.einsum('bsf,fd->bsd', u, w_mlp_out[l])
    return x


def setup_inputs(seed=0):
    out = dict(first_inputs(seed))
    for name, value in second_inputs(seed + 1).items():
        if name != "x":
            out[name + "_2"] = value
    return out


def reference(
    x, mem, rel_bias, mem_norm_g, norm_mix_g, norm_xattn_g, norm_mlp_g, final_norm_g, ab_w_in,
    ab_w_out, lambda_q1, lambda_k1, lambda_q2, lambda_k2, subln_g, pool_w, pool_scale,
    conv_w_in, conv_w, conv_w_out, xattn_wq, xattn_wkv, xattn_wo, mlp_w1, mlp_w2, c_2, w_ada_2,
    b_ada_2, w_in_2, b_forget_2, q_norm_gain_2, k_norm_gain_2, fox_out_gain_2, ret_out_gain_2,
    w_out_2, w_mlp_in_2, w_mlp_out_2,
):
    x = first_block(
        x, mem, rel_bias, mem_norm_g, norm_mix_g, norm_xattn_g, norm_mlp_g, final_norm_g,
        ab_w_in, ab_w_out, lambda_q1, lambda_k1, lambda_q2, lambda_k2, subln_g, pool_w,
        pool_scale, conv_w_in, conv_w, conv_w_out, xattn_wq, xattn_wkv, xattn_wo, mlp_w1,
        mlp_w2,
    )
    return second_block(
        x, c_2, w_ada_2, b_ada_2, w_in_2, b_forget_2, q_norm_gain_2, k_norm_gain_2,
        fox_out_gain_2, ret_out_gain_2, w_out_2, w_mlp_in_2, w_mlp_out_2,
    )


_drawn_inputs = setup_inputs


def setup_inputs(seed=0):
    import zlib

    import numpy as np

    out = dict(_drawn_inputs(seed))
    spreads = {}
    factors = {'mem_norm_g': 8.0,
     'norm_xattn_g': 8.0,
     'final_norm_g': 2.728,
     'lambda_q1': 8.0,
     'subln_g': 4.621,
     'q_norm_gain_2': 8.0,
     'k_norm_gain_2': 8.0,
     'fox_out_gain_2': 30.102,
     'ret_out_gain_2': 27.244}
    for name, (base, spread) in spreads.items():
        noise = np.random.default_rng([zlib.crc32(name.encode()), seed]).standard_normal(out[name].shape)
        drawn = base * np.exp(spread * noise) if base else spread * noise
        out[name] = __import__('jax').numpy.asarray(drawn.astype(out[name].dtype))
    for name, factor in factors.items():
        out[name] = (out[name] * factor).astype(out[name].dtype)
    return out
```

```python
from contextlib import ExitStack
import math

import numpy as np

import concourse.bass as bass
from concourse import mybir

F32 = mybir.dt.float32
F32R = mybir.dt.float32r
BF16 = mybir.dt.bfloat16
ALU = mybir.AluOpType
ACT = mybir.ActivationFunctionType
AX_X = mybir.AxisListType.X

P = 128
D = 1024
S = 256
T = S // P
KC = D // P
NB = 512
HC = KC // 2
HALF = HC * NB
RING = 4
EPS = 1e-6
NEG = -1e30
LAMBDA_INIT = 0.8 - 0.6 * math.exp(-0.3 * 0)
BUCKETS, MAX_EXACT, MAX_DIST = 32, 16, 128
WINDOWS = (2, 4, 8, 16)
ADA_COLS = 3
ADA_LOADS = 16

def _blocks(name, cols, row=0):
    return [(name, row, c) for c in cols]


def _mlp(w1, w2):
    out = []
    for j in range(4):
        out += _blocks(w1, (2 * j, 2 * j + 1)) + _blocks(w2, (0, 1), j)
    return out


SECTIONS = [
    ("l0_u", _blocks("ab_in", [3])),
    ("l0_q", _blocks("ab_in", [0])),
    ("l0_k", _blocks("ab_in", [1])),
    ("l0_v", _blocks("ab_in", [2])),
    ("kv0", _blocks("wkv0", [0, 1, 2, 3])),
    ("l0_out", _blocks("ab_out", [0, 1])),
    ("q0", _blocks("wq0", [0, 1])),
    ("o0", _blocks("wo0", [0, 1])),
    ("mlp0", _mlp("w1_0", "w2_0")),
    ("kv1a", _blocks("wkv1", [0])),
    ("conv", _blocks("conv_in", [2, 4, 0, 3, 5, 1])),
    ("kv1b", _blocks("wkv1", [1])),
    ("conv_out", _blocks("conv_out", [0, 1])),
    ("kv1c", _blocks("wkv1", [2])),
    ("q1", _blocks("wq1", [0, 1])),
    ("kv1d", _blocks("wkv1", [3])),
    ("o1", _blocks("wo1", [0, 1])),
    ("mlp1", _mlp("w1_1", "w2_1")),
    ("fq", _blocks("in2", [0])),
    ("fk", _blocks("in2", [1])),
    ("fv", _blocks("in2", [2])),
    ("rq", _blocks("in2", [4])),
    ("rk", _blocks("in2", [5])),
    ("rv", _blocks("in2", [6])),
    ("fog", _blocks("in2", [3])),
    ("rg", _blocks("in2", [7])),
    ("out2", _blocks("out2", [0, 1])),
    ("mlp2", _mlp("w1_2", "w2_2")),
]
UNIT = {}
UNITS = []
for _name, _list in SECTIONS:
    UNIT[_name] = len(UNITS)
    UNITS += _list
NU = len(UNITS)
NH = 2 * NU

NORMS = ["mix0", "mem", "x0", "mlp0", "mix1", "x1", "mlp1", "mix2", "mlp2"]
STATS = NORMS[:7] + ["final"] + NORMS[7:]
GAINS = ["mix0", "mem", "x0", "mlp0", "mix1", "x1", "mlp1", "final"]


class Signal:

    def __init__(self, sem, labels):
        self.sem = sem
        self.order = list(labels)
        self.value = {label: n + 1 for n, label in enumerate(self.order)}
        self.raised = 0

    def at(self, label):
        return self.sem, self.value[label]

    def up(self, label):
        assert self.order[self.raised] == label, (self.order[self.raised], label)
        self.raised += 1
        return self.sem, 1


def constants():
    f = np.float32
    c = {}
    c["ident"] = np.eye(P, dtype=f)
    c["ones"] = np.ones((P, P), f)
    c["flip"] = np.eye(P, dtype=f)[::-1].copy()
    dist = np.maximum(S - 1 - np.arange(384), 0)
    nf = np.maximum(dist, 1).astype(f)
    large = MAX_EXACT + (np.log(nf / f(MAX_EXACT)) / f(math.log(MAX_DIST / MAX_EXACT))
                         * f(BUCKETS - MAX_EXACT)).astype(np.int32)
    bucket = np.where(dist < MAX_EXACT, dist, np.minimum(large, BUCKETS - 1))
    c["bucket"] = (np.arange(BUCKETS)[:, None] == bucket[None, :]).astype(f)
    t = np.arange(S)
    pool = np.zeros((S, len(WINDOWS), S), f)
    for g, w in enumerate(WINDOWS):
        inside = (t[None, :] >= t[:, None]) & (t[None, :] - t[:, None] < w)
        pool[:, g, :] = inside / np.minimum(t + 1, w).astype(f)[None, :] - np.eye(S, dtype=f)
    c["pool"] = pool.reshape(T, P, len(WINDOWS), S).transpose(1, 0, 2, 3).reshape(P, -1)
    half = np.arange(P) // 64
    block = (half[:, None] == half[None, :]).astype(f)
    rot = np.zeros((P, P), f)
    for d in range(64):
        rot[d + 64, d] = -1.0
        rot[d, d + 64] = 1.0
    tri = (np.arange(P)[:, None] <= np.arange(P)[None, :]).astype(f)
    freq = f(10000.0) ** (-np.arange(0, P, 2, dtype=f) / f(P))
    ang = (np.arange(S, dtype=f)[None, :] * np.concatenate([freq, freq])[:, None]).astype(f)
    c["second"] = np.concatenate([block, rot, tri, np.cos(ang), np.sin(ang)], axis=1).astype(f)
    log_g = np.log(1.0 - 2.0 ** (-5.0 - np.arange(4, dtype=np.float64)))
    diff = np.arange(S)[None, :] - np.arange(P)[:, None]
    decay = np.where(diff[:, None, :] >= 0,
                     np.exp(np.maximum(diff, 0)[:, None, :] * log_g[None, :, None]), 0.0)
    c["decay"] = (decay * 128.0 ** -0.5).astype(f).reshape(P, -1)
    return {k: np.ascontiguousarray(v, dtype=f) for k, v in c.items()}


COL = {}
_at = 0
for _name, _n in (("subln", 1), ("pool_scale", 4), ("conv", 24), ("qg", 1), ("kg", 1), ("foxg", 4),
                  ("retg", 4), ("b_ada", 48), ("b_forget", 8)):
    COL[_name] = slice(_at, _at + _n)
    _at += _n
N_COLS = _at


def build(nc, d, out):
    ctx = ExitStack()
    with ctx:
        program(nc, ctx, d, out)


def program(nc, ctx, d, out):
    def sb(name, shape, dt=F32):
        return ctx.enter_context(nc.sbuf_tensor(name, shape, dt))

    def sem(name):
        return ctx.enter_context(nc.semaphore(name))

    def signal(name, labels):
        return Signal(sem(name), labels)

    raw = sb("raw", [P, RING, HC, NB])
    hi = sb("hi", [P, RING, HC, NB], F32R)
    lo = sb("lo", [P, RING, HC, NB], F32R)
    xt_hi = sb("xt_hi", [P, KC, S], F32R)
    xt_lo = sb("xt_lo", [P, KC, S], F32R)
    yt_hi = sb("yt_hi", [P, KC, S], F32R)
    yt_lo = sb("yt_lo", [P, KC, S], F32R)
    mt_hi = sb("mt_hi", [P, KC, S], F32R)
    mt_lo = sb("mt_lo", [P, KC, S], F32R)
    h = sb("h", [P, T, D])
    hn = sb("hn", [P, T, D])
    work = sb("work", [P, 11264])
    ident = sb("ident", [P, P])
    ones = sb("ones", [P, P])
    cols = sb("cols", [P, N_COLS])
    mod = sb("mod", [P, 48])
    mod_part = sb("mod_part", [P, 2 * ADA_COLS])
    stat = sb("stat", [P, 2 * len(STATS)])
    rstd = sb("rstd", [P, 2 * len(STATS)])
    power = sb("power", [P, 1])
    eps = sb("eps", [P, 1])
    peak = sb("peak", [P, 16])
    shift = sb("shift", [P, 16])
    total = sb("total", [P, 16])
    inv = sb("inv", [P, 16])
    lam = sb("lam", [P, 8])
    mask_bf = sb("mask_bf", [P, P], BF16)
    ident_bf = sb("ident_bf", [P, P], BF16)
    ff_raw = sb("ff_raw", [P, KC, 8])
    ff_hi = sb("ff_hi", [P, KC, 8], F32R)
    ff_lo = sb("ff_lo", [P, KC, 8], F32R)
    logf = sb("logf", [P, 6, 2 * 8])
    gemm = ctx.enter_context(nc.psum_tensor("gemm", [P, 4, NB], F32))
    bank = ctx.enter_context(nc.psum_tensor("bank", [P, 4, NB], F32))

    def w(start, *shape):
        n = int(np.prod(shape))
        flat = work[:, start:start + n]
        if len(shape) == 2:
            return flat.rearrange("p (a b) -> p a b", a=shape[0])
        if len(shape) == 3:
            return flat.rearrange("p (a b c) -> p a b c", a=shape[0], b=shape[1])
        return flat

    def cut(ap, a):
        return ap.rearrange("p (a b) -> p a b", a=a)

    def flat(ap):
        return ap.rearrange("p a b -> p (a b)")

    def col(name, n=0):
        return cols[:, COL[name].start + n:COL[name].start + n + 1]

    q_t, k_t, v_nat = w(0, 4, S), w(1024, 4, S), w(2048, T, NB)
    bias1, bias0 = w(3072, 4, S), w(4096, 4, P)
    flip1, flip0 = w(0, 4, S), w(1024, 4, P)
    kv_k, kv_v = w(5120, KC, S), w(7168, T, D)
    mem_rows = w(7168, T, D)
    u_nat, pool_y, lam_in = w(2048, T, NB), w(2048, 4, S), w(2048, 4, 64)
    pool_w, pool_m = w(4608, 4, P), w(5120, T, 4, S)
    gain = w(9216, D)
    pool_t, a_t = w(10240, 4, S), w(10240, 2, 4, P)
    flip_m, bucket_m, rel, bias_row = w(10240, P), w(10368, 384), w(10752, 4), w(10756, 384)
    diff_o, diff_sq, diff_r = w(0, 4, S), w(1024, 4, S), w(3072, 4, S)
    cq_t, p_t = w(0, KC, S), w(2048, 2, 4, P)
    ada, c_tmp, c_act = w(0, ADA_COLS, D), w(3072, D), w(4096, D)
    gate_c, z_pad, conv_y = w(0, 4, S), w(1024, 4, S + 2), w(2056, 4, S)
    fq_t, fk_t, fv_nat, fog_t = w(0, 4, S), w(1024, 4, S), w(2048, T, NB), w(3072, 4, S)
    rq_t, rk_t, rv_nat, rg_t = w(4096, 4, S), w(5120, 4, S), w(6144, T, NB), w(7168, 4, S)
    rg_exp_t, rope_tmp = w(2048, 4, S), w(7168, 4, S)
    const2 = w(8192, 896)
    block_m, rot_m, tri_m = const2[:, 0:128], const2[:, 128:256], const2[:, 256:384]
    cos_m, sin_m = const2[:, 384:640], const2[:, 640:896]
    cum_rows = w(3072, S)[0:8]
    decay_m, shift_row, e_t = w(9216, 4, S), w(10240, D), w(10240, 8, P)
    gate_m_row, gate_f_row, gated = w(1024, D), w(3072, D), w(5120, T, NB)

    rows_dram = nc.dram_tensor("bias_rows", (4, 384), F32, kind="Internal").ap()

    landed = [sem(f"half_landed{n}") for n in range(RING)]
    hi_ready, lo_ready = sem("hi_ready"), sem("lo_ready")
    half_used = sem("half_used")
    bank0_done = sem("bank0_done")
    evacuated = [sem(f"set_evacuated{n}") for n in range(2)]
    filled = [sem(f"bank_filled{n}") for n in range(4)]
    freed = [sem(f"bank_freed{n}") for n in range(4)]
    hid_hi = [sem(f"hidden_hi{m}") for m in range(3)]
    hid_sq = [sem(f"hidden_square{m}") for m in range(3)]
    hid_ready = [sem(f"hidden_ready{m}") for m in range(3)]
    gated_done = sem("gated_done")
    ada_landed, ada_used, ada_kept = sem("ada_landed"), sem("ada_used"), sem("ada_kept")
    loads = (["x", "mem", "consts", "rel", "lam", "pool", "flipped", "c", "ff", "const2", "decay"]
             + ["gain_" + g for g in GAINS])
    loaded = {name: sem("loaded_" + name) for name in loads}
    bias_stored, out_stored = sem("bias_stored"), sem("out_stored")

    stat_tiles = [(n, t) for n in STATS for t in range(T)]
    norm_tiles = [(n, t) for n in NORMS for t in range(T)]
    squares = signal("squares_summed", stat_tiles)
    mean_done = signal("mean_done", stat_tiles)
    rstd_done = signal("rstd_done", stat_tiles)
    final_done = signal("final_norm_done", range(T))
    normed = signal("normed", norm_tiles)
    turned_hi = signal("transposed_hi", [(n, t, j) for n, t in norm_tiles for j in range(2)])
    vec_step, act_step = sem("vector_step"), sem("scalar_step")
    set_up = sem("constants_set")
    bias_masked = signal("bias_masked", [0, 1])
    pool_y_ready = signal("pool_y_ready", [0, 1])
    YT = [("pool", 0), ("pool", 1), ("diff", 0), ("diff", 1), ("conv", 0), ("conv", 1), "fo", "ro"]
    yt_ready = signal("yt_ready", YT)
    yt_hi_ready = signal("yt_hi_ready", YT[0:4] + [("x0", g) for g in range(4)] + YT[4:6]
                         + [("x1", g) for g in range(4)] + YT[6:8])
    lam_sums, lam_exp, lam_ready = (signal("lambda_sums", [0, 1]), signal("lambda_exp", [0, 1]),
                                    signal("lambda_ready", [0]))
    GROUPS = [(name, g) for name in ("d", "x0", "x1", "f") for g in range(4)]
    shift_ready = signal("shift_ready", GROUPS)
    diff_exp = signal("diff_exp", range(4))
    probs_ready = signal("probs_ready", GROUPS)
    HEADS = ["d0", "d1", "fq", "fk", "fo", "ro"]
    hsq = signal("head_squares", HEADS)
    hnormed = signal("head_normed", HEADS)
    c_exp = signal("c_exp", [0])
    mod_ready = signal("mod_ready", [0])
    conv_z, conv_y_ready = signal("conv_z", [0, 1]), signal("conv_y", [0, 1])
    ff_hi_ready, ff_ready = signal("ff_hi", [0]), signal("ff_ready", [0])
    logf_abs, logf_ln, logf_ready = (signal("logf_abs", [0]), signal("logf_ln", [0]),
                                     signal("logf_ready", [0]))
    roped = signal("roped", ["q", "k"])
    decayed = signal("decayed", range(4))
    rg_kept, rg_exp = signal("rg_kept", [0]), signal("rg_exp", [0])

    fills = {}
    bank_uses = [0, 0, 0, 0]

    def fill(label):
        n, k = fills[label]
        return filled[n], k

    def read(label):
        n, k = fills[label]
        return freed[n], k

    def set_done(u, tiles=2):
        return evacuated[u % 2], 2 * (u // 2) + tiles

    block = ctx.enter_context(nc.Block())

    @block.sync
    def _(sp):
        for s in range(RING):
            sp.dma_start(raw[:, s], d["weights"][s]).then_inc(landed[s], 16)
        with sp.Fori(1, NH // RING) as i:
            for s in range(RING):
                sp.wait_ge(lo_ready, RING * i + (s - RING + 1))
                sp.dma_start(raw[:, s], d["weights"][RING * i + s]).then_inc(landed[s], 16)
        for t in range(T):
            sp.wait_ge(*set_done(NU - 1, t + 1))
            sp.dma_start(out[t * P:(t + 1) * P, :], h[:, t, :]).then_inc(out_stored, 16)
        sp.wait_ge(out_stored, 16 * T)

    @block.tensor
    def _(pe):
        XT, YT_, MT = (xt_hi, xt_lo), (yt_hi, yt_lo), (mt_hi, mt_lo)

        def claim(n, label):
            if bank_uses[n]:
                pe.wait_ge(freed[n], bank_uses[n])
            bank_uses[n] += 1
            fills[label] = (n, bank_uses[n])

        def unit(u, x, stationary, waits=(None, None), i=None):
            s = u % 2
            if u >= 2:
                pe.wait_ge(evacuated[s], 2 * (u // 2) + (0 if i is None else 4 * i))
            for b in range(2):
                slot = (2 * u + b) % RING
                pe.wait_ge(lo_ready, 2 * u + b + 1 + (0 if i is None else 8 * i))
                if waits[b] is not None:
                    pe.wait_ge(*waits[b])
                pairs = ((x[0], hi), (x[0], lo), (x[1], hi))
                if stationary == "x":
                    for t in range(T):
                        for k in range(HC):
                            c = b * HC + k
                            for n, (xs, ws) in enumerate(pairs):
                                mm = pe.matmul(gemm[:, 2 * s + t, :], xs[:, c, t * P:(t + 1) * P],
                                               ws[:, slot, k, :], start=(c == 0 and n == 0),
                                               stop=(c == KC - 1 and n == 2), skip_group_check=True)
                        if b == 1 and t == 0:
                            mm.then_inc(bank0_done, 1)
                else:
                    for j in range(4):
                        o = gemm[:, 2 * s + j // 2, (j % 2) * S:(j % 2 + 1) * S]
                        for k in range(HC):
                            c = b * HC + k
                            for n, (xs, ws) in enumerate(pairs):
                                mm = pe.matmul(o, ws[:, slot, k, j * P:(j + 1) * P], xs[:, c, :],
                                               start=(c == 0 and n == 0 and j % 2 == 0),
                                               stop=(c == KC - 1 and n == 2), skip_group_check=True)
                        if b == 1 and j == 1:
                            mm.then_inc(bank0_done, 1)
                mm.then_inc(half_used, 1)

        def transposes(n):
            for t in range(T):
                pe.wait_ge(*normed.at((n, t)))
                for j in range(2):
                    claim(2 + j, (n, t, j))
                    for k in range(HC):
                        c = j * HC + k
                        mm = pe.transpose(bank[:, 2 + j, k * P:(k + 1) * P],
                                          hn[:, t, c * P:(c + 1) * P], ident[:, :])
                    mm.then_inc(filled[2 + j], 1)

        def split(n):
            return read((n, T - 1, 0)), read((n, T - 1, 1))

        def turn_probs(grp, e, heads, tiles, part=0):
            claim(2, ("t", grp, part))
            for n, (a, b) in enumerate([(a, b) for a in heads for b in tiles]):
                mm = pe.transpose(bank[:, 2, n * P:(n + 1) * P], e[:, a, b * P:(b + 1) * P], ident[:, :])
            mm.then_inc(filled[2], 1)

        def head_sums(name, matrix, sq):
            pe.wait_ge(*hsq.at(name))
            for b in range(len(sq)):
                claim(b, ("h", name, b))
                pe.matmul(bank[:, b, :], matrix, sq[b], start=True, stop=True).then_inc(filled[b], 1)

        def row(name, index, first):
            for j in range(2):
                claim(first + j, ("row", name, j))
                for k in range(HC):
                    m = index * KC + j * HC + k
                    mm = pe.matmul(bank[:, first + j, k * P:(k + 1) * P],
                                   mod[:, m:m + 1].to_broadcast((P, P)), ident[:, :],
                                   start=True, stop=True, skip_group_check=True)
                mm.then_inc(filled[first + j], 1)

        def out_units(name, w0, w1):
            unit(UNIT[name], YT_, "x", (w0, w1))
            unit(UNIT[name] + 1, YT_, "x")

        pe.wait_ge(loaded["consts"], 48)
        pe.wait_ge(loaded["rel"], 48)
        claim(0, "bias_row")
        pe.matmul(bank[0:4, 0, 0:384], rel[0:BUCKETS, :], bucket_m[0:BUCKETS, :], start=True, stop=True)\
            .then_inc(filled[0], 1)
        transposes("mix0")
        unit(UNIT["l0_u"], XT, "x", split("mix0"))
        pe.wait_ge(loaded["flipped"], 32)
        for n, src in ((0, flip1[:, 0:2, :]), (1, flip1[:, 2:4, :]), (2, flip0)):
            claim(n, ("bias", n))
            pe.matmul(bank[:, n, :], flip_m, flat(src), start=True, stop=True).then_inc(filled[n], 1)
        unit(UNIT["l0_q"], XT, "w")
        transposes("mem")
        pe.wait_ge(loaded["pool"], 32)
        pe.wait_ge(*set_done(UNIT["l0_u"]))
        for g in range(4):
            n = g // 2
            if g % 2 == 0:
                claim(n, ("pool_t", n))
            for t in range(T):
                mm = pe.matmul(bank[:, n, (g % 2) * S:(g % 2 + 1) * S], u_nat[:, t, g * P:(g + 1) * P],
                               pool_m[:, t, g, :], start=(t == 0), stop=(t == T - 1), skip_group_check=True)
            if g % 2 == 1:
                mm.then_inc(filled[n], 1)
        unit(UNIT["l0_k"], XT, "w")
        for g in range(4):
            n = g // 2
            if g % 2 == 0:
                pe.wait_ge(*read(("pool_t", n)))
                claim(2 + n, ("pool_y", n))
            mm = pe.matmul(bank[:, 2 + n, (g % 2) * S:(g % 2 + 1) * S], pool_w[:, g, :], pool_t[:, g, :],
                           start=True, stop=True, skip_group_check=True)
            if g % 2 == 1:
                mm.then_inc(filled[2 + n], 1)
        unit(UNIT["l0_v"], XT, "x")

        pe.wait_ge(*set_done(UNIT["l0_q"]))
        pe.wait_ge(*set_done(UNIT["l0_k"]))
        for g in range(4):
            hg, qt = g // 2, g % 2
            nk = P * (qt + 1)
            for s in range(2):
                claim(s, ("s", ("d", g), s))
                r = slice(64 * s, 64 * s + 64)
                for a in range(2):
                    mm = pe.matmul(bank[:, s, a * S:a * S + nk], q_t[r, 2 * hg + a, qt * P:(qt + 1) * P],
                                   k_t[r, 2 * hg + a, 0:nk], start=True, stop=True, skip_group_check=True)
                mm.then_inc(filled[s], 1)
            unit(UNIT["kv0"] + g, MT, "w" if g < 2 else "x", split("mem") if g == 0 else (None, None))
            if g == 0:
                pe.wait_ge(*set_done(UNIT["l0_v"]))
            pe.wait_ge(*probs_ready.at(("d", g)))
            turn_probs(("d", g), cut(hn[:, g % 2, 0:2 * S], 2), range(2), range(qt + 1))
            pe.wait_ge(*read(("t", ("d", g), 0)))
            if qt == 0:
                claim(3, ("o", ("d", hg)))
            for a in range(2):
                for kt in range(qt + 1):
                    mm = pe.matmul(bank[:, 3, a * S + qt * P:a * S + (qt + 1) * P],
                                   v_nat[:, kt, (2 * hg + a) * P:(2 * hg + a + 1) * P],
                                   a_t[:, g % 2, a * (qt + 1) + kt, :],
                                   start=(kt == 0), stop=(kt == qt), skip_group_check=True)
            if qt == 1:
                mm.then_inc(filled[3], 1)
        for b in range(2):
            pe.wait_ge(*hsq.at(f"d{b}"))
            claim(b, ("h", f"d{b}", 0))
            pe.matmul(bank[:, b, :], ones[:, :], flat(diff_sq[:, 2 * b:2 * b + 2, :]), start=True,
                      stop=True).then_inc(filled[b], 1)
        out_units("l0_out", yt_ready.at(("pool", 1)), yt_ready.at(("diff", 1)))

        def cross(x, filler=None):
            u = UNIT["q" + x[1]]
            unit(u, XT, "w", split(x))
            unit(u + 1, XT, "w")

            def scores(g):
                qt, hg = g // 2, g % 2
                pe.wait_ge(*set_done(u + hg))
                claim(g % 2, ("s", (x, g), 0))
                for a in range(2):
                    for dc in range(2):
                        c = (2 * hg + a) * 2 + dc
                        mm = pe.matmul(bank[:, g % 2, a * S:(a + 1) * S], cq_t[:, c, qt * P:(qt + 1) * P],
                                       kv_k[:, c, :], start=(dc == 0), stop=(dc == 1), skip_group_check=True)
                mm.then_inc(filled[g % 2], 1)

            scores(0)
            scores(1)
            if filler is not None:
                unit(UNIT[filler], MT, "x")
                pe.wait_ge(*set_done(UNIT[filler]))
            for g in range(4):
                hg = g % 2
                pe.wait_ge(*probs_ready.at((x, g)))
                turn_probs((x, g), cut(hn[:, g // 2, (g % 2) * NB:(g % 2 + 1) * NB], 2), range(2), range(2))
                if g + 2 < 4:
                    scores(g + 2)
                pe.wait_ge(*read(("t", (x, g), 0)))
                claim(3, ("o", (x, g)))
                for a in range(2):
                    for dc in range(2):
                        c = (2 * hg + a) * 2 + dc
                        for mt in range(2):
                            mm = pe.matmul(bank[:, 3, (2 * a + dc) * P:(2 * a + dc + 1) * P],
                                           kv_v[:, mt, c * P:(c + 1) * P], p_t[:, g % 2, 2 * a + mt, :],
                                           start=(mt == 0), stop=(mt == 1), skip_group_check=True)
                mm.then_inc(filled[3], 1)
            out_units("o" + x[1], read(("o", (x, 2))), read(("o", (x, 3))))

        def mlp(m, n):
            u0 = UNIT[f"mlp{m}"]
            pe.wait_ge(*split(n)[0])
            pe.wait_ge(*split(n)[1])
            with pe.Fori(0, 4) as i:
                unit(u0, XT, "w", i=i)
                unit(u0 + 1, XT, "w", i=i)
                unit(u0 + 2, YT_, "x", ((hid_ready[m], 2 * i + 1), (hid_ready[m], 2 * i + 2)), i=i)
                unit(u0 + 3, YT_, "x", i=i)

        transposes("x0")
        cross("x0")
        transposes("mlp0")
        mlp(0, "mlp0")
        unit(UNIT["kv1a"], MT, "w")
        transposes("mix1")
        for n in range(6):
            unit(UNIT["conv"] + n, XT, "w", split("mix1") if n == 0 else (None, None))
        unit(UNIT["kv1b"], MT, "w")
        out_units("conv_out", yt_ready.at(("conv", 0)), yt_ready.at(("conv", 1)))
        unit(UNIT["kv1c"], MT, "x")
        transposes("x1")
        cross("x1", "kv1d")
        transposes("mlp1")
        mlp(1, "mlp1")

        pe.wait_ge(*mod_ready.at(0))
        row("scale_m", 1, 0)
        row("shift_m", 0, 0)
        transposes("mix2")
        unit(UNIT["fq"], XT, "w", split("mix2"))
        unit(UNIT["fk"], XT, "w")
        pe.wait_ge(loaded["const2"], 16)
        head_sums("fq", block_m, [hn[:, 0, 0:NB], hn[:, 0, NB:D]])
        pe.wait_ge(*ff_ready.at(0))
        claim(2, "ff")
        for t in range(T):
            for c in range(KC):
                for n, (xs, ws) in enumerate(((xt_hi, ff_hi), (xt_hi, ff_lo), (xt_lo, ff_hi))):
                    mm = pe.matmul(bank[:, 2, t * 8:(t + 1) * 8], xs[:, c, t * P:(t + 1) * P], ws[:, c, :],
                                   start=(c == 0 and n == 0), stop=(c == KC - 1 and n == 2),
                                   skip_group_check=True)
        mm.then_inc(filled[2], 1)
        unit(UNIT["fv"], XT, "x")
        head_sums("fk", block_m, [hn[:, 1, 0:NB], hn[:, 1, NB:D]])
        pe.wait_ge(*logf_ready.at(0))
        claim(2, "cum")
        lf0, lf1 = logf[:, 4, 0:8], logf[:, 4, 8:16]
        for o, terms in ((bank[:, 2, 0:8], [(tri_m, lf0)]),
                         (bank[:, 2, 8:16], [(ones[:, :], lf0), (tri_m, lf1)]),
                         (bank[0:8, 2, 128:256], [(lf0, tri_m)]),
                         (bank[0:8, 2, 256:384], [(lf0, ones[:, :]), (lf1, tri_m)])):
            for n, (a, b) in enumerate(terms):
                mm = pe.matmul(o, a, b, start=(n == 0), stop=(n == len(terms) - 1), skip_group_check=True)
        mm.then_inc(filled[2], 1)

        def fox_scores(g):
            hg, qt = g // 2, g % 2
            nk = P * (qt + 1)
            for b in range(2):
                claim(b, ("s", ("f", g), b))
                r = slice(64 * b, 64 * b + 64)
                for a in range(2):
                    c = 2 * hg + a
                    o = bank[:, b, a * S:a * S + nk]
                    pe.matmul(o, fq_t[r, c, qt * P:(qt + 1) * P], fk_t[r, c, 0:nk], start=True, stop=False,
                              skip_group_check=True)
                    pe.matmul(o, ident[0:8, 2 * c + b:2 * c + b + 1].to_broadcast((8, P)), cum_rows[:, 0:nk],
                              start=False, stop=False, skip_group_check=True)
                    mm = pe.matmul(bank[:, b, a * S + qt * P:a * S + (qt + 1) * P], ident_bf[:, :],
                                   mask_bf[:, :], start=False, stop=True, skip_group_check=True)
                mm.then_inc(filled[b], 1)

        def fox_values(g):
            hg, qt = g // 2, g % 2
            e = cut(hn[:, g % 2, :], 4)
            pe.wait_ge(*probs_ready.at(("f", g)))
            for part in range(qt + 1):
                turn_probs(("f", g), e, range(4) if qt == 0 else range(2 * part, 2 * part + 2),
                           range(qt + 1), part)
            if qt == 0:
                claim(3, ("o", ("f", hg)))
            for a in range(4):
                if a == 0 or (a == 2 and qt == 1):
                    pe.wait_ge(*read(("t", ("f", g), a // 2)))
                r = slice(64 * (a // 2), 64 * (a // 2) + 64)
                hd = 4 * hg + 2 * (a % 2) + a // 2
                for kt in range(qt + 1):
                    mm = pe.matmul(bank[r, 3, (a % 2) * S + qt * P:(a % 2) * S + (qt + 1) * P],
                                   fv_nat[:, kt, hd * 64:(hd + 1) * 64], e_t[:, a * (qt + 1) + kt, :],
                                   start=(kt == 0), stop=(kt == qt), skip_group_check=True)
            if qt == 1:
                mm.then_inc(filled[3], 1)

        def rotated(name, src, u):
            pe.wait_ge(*set_done(UNIT[u]))
            for b in range(2):
                claim(b, ("rot", name, b))
                pe.matmul(bank[:, b, :], rot_m, flat(src[:, 2 * b:2 * b + 2, :]), start=True, stop=True)\
                    .then_inc(filled[b], 1)

        pe.wait_ge(*hnormed.at("fk"))
        pe.wait_ge(*read("cum"))
        fox_scores(0)
        unit(UNIT["rq"], XT, "w")
        pe.wait_ge(*set_done(UNIT["fv"]))
        fox_values(0)
        fox_scores(1)
        unit(UNIT["rk"], XT, "w")
        fox_values(1)
        rotated("q", rq_t, "rq")
        fox_scores(2)
        unit(UNIT["rv"], XT, "x")
        fox_values(2)
        rotated("k", rk_t, "rk")
        fox_scores(3)
        unit(UNIT["fog"], XT, "w")
        fox_values(3)
        pe.wait_ge(*roped.at("k"))
        pe.wait_ge(*set_done(UNIT["rv"]))

        def ret_scores(a):
            claim(a % 2, ("rs", a))
            pe.matmul(bank[:, a % 2, 0:S], rk_t[:, a, 0:P], rq_t[:, a, :], start=True, stop=True,
                      skip_group_check=True)
            pe.matmul(bank[:, a % 2, S:S + P], rk_t[:, a, P:S], rq_t[:, a, P:S], start=True, stop=True,
                      skip_group_check=True).then_inc(filled[a % 2], 1)

        ret_scores(0)
        ret_scores(1)
        unit(UNIT["rg"], XT, "w")
        for a in range(4):
            n = 2 + a // 2
            pe.wait_ge(*decayed.at(a))
            if a % 2 == 0:
                claim(n, ("o", ("r", a // 2)))
            st = hn[:, a // 2, (a % 2) * NB:(a % 2) * NB + S + P]
            pe.matmul(bank[:, n, (a % 2) * S:(a % 2 + 1) * S], rv_nat[:, 0, a * P:(a + 1) * P], st[:, 0:S],
                      start=True, stop=False, skip_group_check=True)
            mm = pe.matmul(bank[:, n, (a % 2) * S + P:(a % 2 + 1) * S], rv_nat[:, 1, a * P:(a + 1) * P],
                           st[:, S:S + P], start=False, stop=True, skip_group_check=True)
            if a % 2 == 1:
                mm.then_inc(filled[n], 1)
            if a < 2:
                ret_scores(a + 2)
        head_sums("fo", block_m, [flat(fk_t[:, 0:2, :]), flat(fk_t[:, 2:4, :])])
        head_sums("ro", ones[:, :], [flat(rk_t[:, 0:2, :]), flat(rk_t[:, 2:4, :])])
        row("gate_m", 2, 2)
        row("scale_f", 4, 2)
        row("shift_f", 3, 2)
        row("gate_f", 5, 2)
        out_units("out2", yt_ready.at("fo"), yt_ready.at("ro"))
        transposes("mlp2")
        mlp(2, "mlp2")

    @block.scalar
    def _(act):
        steps = [0]

        def step(ins):
            steps[0] += 1
            ins.then_inc(act_step, 1)
            act.wait_ge(act_step, steps[0])

        def hi_half(k, i=None, last=False):
            if k + (24 if last else 0) >= NH:
                return
            s = k % RING
            i = 3 if last else (0 if i is None else i)
            act.wait_ge(landed[s], 16 * (k // RING + 1) + 32 * i)
            if k >= RING:
                act.wait_ge(half_used, k - RING + 1 + 8 * i)
            act.activation(hi[:, s], raw[:, s], ACT.Copy).then_inc(hi_ready, 1)

        def copy0(u, dst):
            hi_half(2 * u + 4)
            act.wait_ge(bank0_done, u + 1)
            src = gemm[:, 2 * (u % 2), :]
            act.activation(dst, cut(src, 2) if len(dst.shape) == 3 else src, ACT.Copy)\
                .then_inc(evacuated[u % 2], 1)
            hi_half(2 * u + 5)

        def stream(u):
            hi_half(2 * u + 4)
            hi_half(2 * u + 5)

        def sum_squares(n, t, src):
            c = squares.order.index((n, t))
            act.activation(hn[:, t, :], src, ACT.Square, accum_out=stat[:, c:c + 1])\
                .then_inc(*squares.up((n, t)))

        def residual_squares(n, u):
            for t in range(T):
                act.wait_ge(*set_done(u, t + 1))
                sum_squares(n, t, h[:, t, :])

        def turned_hi_parts(n, dst):
            for t in range(T):
                for j in range(2):
                    act.wait_ge(*fill((n, t, j)))
                    act.activation(dst[:, j * HC:(j + 1) * HC, t * P:(t + 1) * P], cut(bank[:, 2 + j, :], HC),
                                   ACT.Copy).then_inc(*turned_hi.up((n, t, j)))

        def keep_turned(grp, dst, part=0):
            act.wait_ge(*fill(("t", grp, part)))
            n = dst.shape[1]
            act.activation(dst, cut(bank[:, 2, :], 4)[:, 0:n, :], ACT.Copy).then_inc(freed[2], 1)

        def keep_row(name, dst, first, bias=0.0):
            for j in range(2):
                act.wait_ge(*fill(("row", name, j)))
                act.activation(dst[:, j * NB:(j + 1) * NB], bank[:, first + j, :], ACT.Copy, bias=bias)\
                    .then_inc(freed[first + j], 1)

        def split_hi(label, dst, src, *wait):
            act.wait_ge(*wait)
            act.activation(dst, src, ACT.Copy).then_inc(*yt_hi_ready.up(label))

        act.wait_ge(loaded["x"], 32)
        for k in range(RING):
            if k < T:
                sum_squares("mix0", k, h[:, k, :])
            hi_half(k)
        act.wait_ge(*fill("bias_row"))
        act.activation(bias_row[0:4, :], bank[0:4, 0, 0:384], ACT.Copy).then_inc(freed[0], 1)
        turned_hi_parts("mix0", xt_hi)
        act.wait_ge(*lam_sums.at(1))
        for n in range(2):
            act.activation(lam[:, 2 + n:3 + n], lam[:, n:n + 1], ACT.Exp).then_inc(*lam_exp.up(n))
        act.wait_ge(loaded["mem"], 32)
        for t in range(T):
            act.wait_ge(*fill(("mix0", t, 1)))
            sum_squares("mem", t, mem_rows[:, t, :])
        copy0(UNIT["l0_u"], u_nat[:, 0, :])
        copy0(UNIT["l0_q"], q_t[:, 0:2, :])
        turned_hi_parts("mem", mt_hi)
        for b in range(2):
            act.wait_ge(*fill(("pool_t", b)))
            act.activation(pool_t[:, 2 * b:2 * b + 2, :], cut(bank[:, b, :], 2), ACT.Copy)\
                .then_inc(freed[b], 1)
        copy0(UNIT["l0_k"], k_t[:, 0:2, :])
        for b in range(2):
            act.wait_ge(*fill(("pool_y", b)))
            for a in range(2):
                g = 2 * b + a
                ins = act.activation(pool_y[:, g, :], cut(bank[:, 2 + b, :], 2)[:, a, :], ACT.Copy,
                                     scale=col("pool_scale", g))
            ins.then_inc(freed[2 + b], 1)
            split_hi(("pool", b), yt_hi[:, 2 * b:2 * b + 2, :], pool_y[:, 2 * b:2 * b + 2, :],
                     *read(("pool_y", b)))
        act.wait_ge(*yt_ready.at(("pool", 1)))
        copy0(UNIT["l0_v"], v_nat[:, 0, :])
        for g in range(4):
            hg, qt = g // 2, g % 2
            nk = P * (qt + 1)
            e = hn[:, g % 2, :].rearrange("p (s a k) -> p s a k", s=2, a=2)
            act.wait_ge(*shift_ready.at(("d", g)))
            for s in range(2):
                for a in range(2):
                    n = 4 * g + 2 * s + a
                    ins = act.activation(e[:, s, a, 0:nk], e[:, s, a, 0:nk], ACT.Exp, bias=shift[:, n:n + 1],
                                         accum_out=total[:, n:n + 1])
            ins.then_inc(*diff_exp.up(g))
            u = UNIT["kv0"] + g
            copy0(u, kv_k[:, 4 * g:4 * g + 2, :] if g < 2 else kv_v[:, 0, (g - 2) * NB:(g - 1) * NB])
            keep_turned(("d", g), a_t[:, g % 2, 0:2 * (qt + 1), :])
            if qt == 1:
                act.wait_ge(*fill(("o", ("d", hg))))
                act.activation(diff_o[:, 2 * hg:2 * hg + 2, :], cut(bank[:, 3, :], 2), ACT.Copy)\
                    .then_inc(freed[3], 1)
        for b in range(2):
            act.wait_ge(*read(("o", ("d", b))))
            act.activation(diff_sq[:, 2 * b:2 * b + 2, :], diff_o[:, 2 * b:2 * b + 2, :], ACT.Square)\
                .then_inc(*hsq.up(f"d{b}"))
        for b in range(2):
            act.wait_ge(*fill(("h", f"d{b}", 0)))
            act.activation(diff_r[:, 2 * b:2 * b + 2, :], cut(bank[:, b, :], 2), ACT.Sqrt, bias=eps[:, :],
                           scale=1.0 / P).then_inc(freed[b], 1)
        for b in range(2):
            split_hi(("diff", b), yt_hi[:, 4 + 2 * b:6 + 2 * b, :], diff_o[:, 2 * b:2 * b + 2, :],
                     *hnormed.at(f"d{b}"))
        stream(UNIT["l0_out"])
        stream(UNIT["l0_out"] + 1)

        def cross(x, filler=None):
            u = UNIT["q" + x[1]]
            for n in range(2):
                copy0(u + n, cq_t[:, 4 * n:4 * n + 2, :])

            def exps(g):
                act.wait_ge(*shift_ready.at((x, g)))
                e = cut(hn[:, g // 2, (g % 2) * NB:(g % 2 + 1) * NB], 2)
                for a in range(2):
                    n = 4 * g + a
                    ins = act.activation(e[:, a, :], cut(bank[:, g % 2, :], 2)[:, a, :], ACT.Exp,
                                         bias=shift[:, n:n + 1], scale=1.0 / 16, accum_out=total[:, n:n + 1])
                ins.then_inc(freed[g % 2], 1)

            exps(0)
            exps(1)
            if filler is not None:
                copy0(UNIT[filler], kv_v[:, 0, NB:D])
            for g in range(4):
                qt, hg = g // 2, g % 2
                keep_turned((x, g), p_t[:, g % 2])
                if g + 2 < 4:
                    exps(g + 2)
                split_hi((x, g), yt_hi[:, 4 * hg:4 * hg + 4, qt * P:(qt + 1) * P], cut(bank[:, 3, :], 4),
                         *fill(("o", (x, g))))
            stream(UNIT["o" + x[1]])
            stream(UNIT["o" + x[1]] + 1)

        def mlp_chunk(m, i, last=False):
            for j in range(4):
                u = UNIT[f"mlp{m}"] + j
                hi_half(2 * u + 4, i, last)
                if j < 2:
                    s = u % 2
                    r = hn[:, j, :]
                    act.wait_ge(bank0_done, u + 1 + 4 * i)
                    act.activation(r[:, 0:NB], gemm[:, 2 * s, :], ACT.Relu).then_inc(evacuated[s], 1)
                    act.wait_ge(half_used, 2 * u + 2 + 8 * i)
                    act.activation(r[:, NB:D], gemm[:, 2 * s + 1, :], ACT.Relu).then_inc(evacuated[s], 1)
                    act.wait_ge(evacuated[s], 2 * (u // 2) + 2 + 4 * i)
                    act.activation(yt_hi[:, 4 * j:4 * j + 4, :], cut(r, 4), ACT.Square)\
                        .then_inc(hid_hi[m], 1)
                hi_half(2 * u + 5, i, last)

        def mlp(m):
            if m < 2:
                with act.Fori(0, 4) as i:
                    mlp_chunk(m, i)
            else:
                with act.Fori(0, 3) as i:
                    mlp_chunk(m, i)
                mlp_chunk(m, 3, last=True)

        residual_squares("x0", UNIT["l0_out"] + 1)
        turned_hi_parts("x0", xt_hi)
        cross("x0")
        act.wait_ge(loaded["c"], 16)
        act.activation(c_tmp, c_act, ACT.Exp, scale=-1.0).then_inc(*c_exp.up(0))
        residual_squares("mlp0", UNIT["o0"] + 1)
        turned_hi_parts("mlp0", xt_hi)
        mlp(0)
        residual_squares("mix1", UNIT["mlp0"] + 15)
        copy0(UNIT["kv1a"], kv_k[:, 0:2, :])
        turned_hi_parts("mix1", xt_hi)
        for b in range(2):
            u = UNIT["conv"] + 3 * b
            if b == 1:
                act.wait_ge(*conv_z.at(0))
            copy0(u, gate_c[:, 0:2, :])
            stream(u + 1)
            stream(u + 2)
            split_hi(("conv", b), yt_hi[:, 4 * b:4 * b + 4, :], conv_y, *conv_y_ready.at(b))
        copy0(UNIT["kv1b"], kv_k[:, 4:6, :])
        stream(UNIT["conv_out"])
        stream(UNIT["conv_out"] + 1)
        residual_squares("x1", UNIT["conv_out"] + 1)
        copy0(UNIT["kv1c"], kv_v[:, 0, 0:NB])
        turned_hi_parts("x1", xt_hi)
        cross("x1", "kv1d")
        residual_squares("mlp1", UNIT["o1"] + 1)
        turned_hi_parts("mlp1", xt_hi)
        mlp(1)

        residual_squares("final", UNIT["mlp1"] + 15)
        for t in range(T):
            act.wait_ge(*final_done.at(t))
            sum_squares("mix2", t, h[:, t, :])
        keep_row("scale_m", gain, 0, bias=1.0)
        keep_row("shift_m", shift_row, 0)
        act.wait_ge(loaded["ff"], 16)
        act.activation(ff_hi[:, :, :], ff_raw[:, :, :], ACT.Copy).then_inc(*ff_hi_ready.up(0))
        turned_hi_parts("mix2", xt_hi)

        def head_squares(name, dst, src, *waits):
            for wait in waits:
                act.wait_ge(*wait)
            act.activation(dst, src, ACT.Square).then_inc(*hsq.up(name))

        def head_roots(name, dst, width):
            for b in range(2):
                act.wait_ge(*fill(("h", name, b)))
                act.activation(dst[:, b * NB:(b + 1) * NB], bank[:, b, :], ACT.Sqrt, bias=eps[:, :],
                               scale=1.0 / width).then_inc(freed[b], 1)

        copy0(UNIT["fq"], fq_t[:, 0:2, :])
        head_squares("fq", hn[:, 0, :], flat(fq_t), set_done(UNIT["fq"]))
        copy0(UNIT["fk"], fk_t[:, 0:2, :])
        head_squares("fk", hn[:, 1, :], flat(fk_t), set_done(UNIT["fk"]))
        head_roots("fq", hn[:, 0, :], 64)
        act.wait_ge(*logf_abs.at(0))
        step(act.activation(logf[:, 2, :], logf[:, 1, :], ACT.Exp, scale=-1.0))
        act.activation(logf[:, 3, :], logf[:, 2, :], ACT.Ln, bias=ones[:, 0:1]).then_inc(*logf_ln.up(0))
        copy0(UNIT["fv"], fv_nat[:, 0, :])
        head_roots("fk", hn[:, 1, :], 64)

        def fox_exps(g):
            qt = g % 2
            nk = P * (qt + 1)
            e = cut(hn[:, g % 2, :], 4)
            act.wait_ge(*shift_ready.at(("f", g)))
            for a in range(4):
                n = 4 * g + a
                ins = act.activation(e[:, a, 0:nk], cut(bank[:, a // 2, :], 2)[:, a % 2, 0:nk], ACT.Exp,
                                     bias=shift[:, n:n + 1], accum_out=total[:, n:n + 1])
                if a % 2 == 1:
                    ins.then_inc(freed[a // 2], 1)

        def fox_kept(g):
            hg, qt = g // 2, g % 2
            for part in range(qt + 1):
                keep_turned(("f", g), e_t[:, 4 * part:4 * part + 4, :], part)
            if qt == 1:
                act.wait_ge(*fill(("o", ("f", hg))))
                act.activation(fq_t[:, 2 * hg:2 * hg + 2, :], cut(bank[:, 3, :], 2), ACT.Copy)\
                    .then_inc(freed[3], 1)

        fox_exps(0)
        copy0(UNIT["rq"], rq_t[:, 0:2, :])
        fox_kept(0)
        fox_exps(1)
        copy0(UNIT["rk"], rk_t[:, 0:2, :])
        fox_kept(1)
        fox_exps(2)
        copy0(UNIT["rv"], rv_nat[:, 0, :])
        fox_kept(2)
        fox_exps(3)
        u = UNIT["fog"]
        hi_half(2 * u + 4)
        for b in range(2):
            act.wait_ge(*((bank0_done, u + 1) if b == 0 else (half_used, 2 * u + 2)))
            act.activation(fog_t[:, 2 * b:2 * b + 2, :], cut(gemm[:, 2 * (u % 2) + b, :], 2), ACT.Exp, scale=-1.0)\
                .then_inc(evacuated[u % 2], 1)
        hi_half(2 * u + 5)
        fox_kept(3)
        head_squares("fo", flat(fk_t), flat(fq_t), read(("o", ("f", 0))), read(("o", ("f", 1))))
        stream(UNIT["rg"])
        act.wait_ge(*rg_kept.at(0))
        act.activation(rg_exp_t, rg_t, ACT.Exp, scale=-1.0).then_inc(*rg_exp.up(0))
        for b in range(2):
            act.wait_ge(*fill(("o", ("r", b))))
            act.activation(rq_t[:, 2 * b:2 * b + 2, :], cut(bank[:, 2 + b, :], 2), ACT.Copy)\
                .then_inc(freed[2 + b], 1)
        head_squares("ro", flat(rk_t), flat(rq_t), read(("o", ("r", 0))), read(("o", ("r", 1))))
        head_roots("fo", flat(fk_t), 64)
        head_roots("ro", flat(rk_t), P)
        split_hi("fo", yt_hi[:, 0:4, :], fq_t, *hnormed.at("fo"))
        split_hi("ro", yt_hi[:, 4:8, :], rq_t, *hnormed.at("ro"))
        keep_row("gate_m", gate_m_row, 2)
        keep_row("scale_f", gain, 2, bias=1.0)
        keep_row("shift_f", shift_row, 2)
        keep_row("gate_f", gate_f_row, 2)
        stream(UNIT["out2"])
        stream(UNIT["out2"] + 1)
        residual_squares("mlp2", UNIT["out2"] + 1)
        turned_hi_parts("mlp2", xt_hi)
        mlp(2)

    @block.vector
    def _(dve):
        steps = [0]
        gate_steps = [0]

        def step(ins, wait=True):
            steps[0] += 1
            ins.then_inc(vec_step, 1)
            if wait:
                dve.wait_ge(vec_step, steps[0])

        def lo_half(k, i=None, last=False):
            if k + (24 if last else 0) >= NH:
                return
            s = k % RING
            i = 3 if last else (0 if i is None else i)
            dve.wait_ge(hi_ready, k + 1 + 8 * i)
            dve.tensor_tensor(lo[:, s], raw[:, s], hi[:, s].bitcast(F32), ALU.subtract).then_inc(lo_ready, 1)

        def copy1(u, dst):
            lo_half(2 * u + 4)
            dve.wait_ge(half_used, 2 * u + 2)
            src = gemm[:, 2 * (u % 2) + 1, :]
            dve.tensor_copy(dst, cut(src, 2) if len(dst.shape) == 3 else src).then_inc(evacuated[u % 2], 1)
            lo_half(2 * u + 5)

        def add_residual(u, n, gate=None, i=None, last=False):
            k = 0 if i is None else i
            lo_half(2 * u + 4, i, last)
            blk = slice(n * NB, (n + 1) * NB)
            for t in range(T):
                dve.wait_ge(*((bank0_done, u + 1 + 4 * k) if t == 0 else (half_used, 2 * u + 2 + 8 * k)))
                src = gemm[:, 2 * (u % 2) + t, :]
                if gate is not None:
                    dve.tensor_tensor(gated[:, t, :], src, gate[:, blk], ALU.mult).then_inc(gated_done, 1)
                    gate_steps[0] += 1
                    dve.wait_ge(gated_done, gate_steps[0] + 4 * k)
                    src = gated[:, t, :]
                dve.tensor_tensor(h[:, t, blk], h[:, t, blk], src, ALU.add).then_inc(evacuated[u % 2], 1)
            lo_half(2 * u + 5, i, last)

        def scaled_rows(n, src):
            for t in range(T):
                c = rstd_done.order.index((n, t))
                dve.wait_ge(*rstd_done.at((n, t)))
                if n == "mix0" or n == "mem" or n in GAINS:
                    dve.wait_ge(loaded["gain_" + n], 16)
                ins = dve.scalar_tensor_tensor(hn[:, t, :], src[:, t, :], rstd[:, c:c + 1], gain, ALU.mult,
                                               ALU.mult)
                if n in ("mix2", "mlp2"):
                    step(ins)
                    ins = dve.tensor_tensor(hn[:, t, :], hn[:, t, :], shift_row, ALU.add)
                ins.then_inc(*normed.up((n, t)))

        def turned_lo_parts(n, dst, upper):
            for t in range(T):
                for j in range(2):
                    dve.wait_ge(*turned_hi.at((n, t, j)))
                    part = (slice(None), slice(j * HC, (j + 1) * HC), slice(t * P, (t + 1) * P))
                    dve.tensor_tensor(dst[part], cut(bank[:, 2 + j, :], HC), upper[part].bitcast(F32),
                                      ALU.subtract).then_inc(freed[2 + j], 1)

        def split_lo(label, part, src):
            dve.wait_ge(*yt_hi_ready.at(label))
            dve.tensor_tensor(yt_lo[part], src, yt_hi[part].bitcast(F32), ALU.subtract)\
                .then_inc(*yt_ready.up(label))

        def recip_total(g, n):
            cs = slice(4 * g, 4 * g + n)
            step(dve.reciprocal(inv[:, cs], total[:, cs]))

        dve.wait_ge(set_up, 4)
        dve.wait_ge(loaded["consts"], 48)
        dve.wait_ge(loaded["lam"], 16)
        for n in range(2):
            dve.tensor_tensor_reduce(lam_in[:, 2 * n, :], lam_in[:, 2 * n, :], lam_in[:, 2 * n + 1, :], 1.0, 0.0,
                                     ALU.mult, ALU.add, lam[:, n:n + 1]).then_inc(*lam_sums.up(n))
        step(dve.tensor_scalar(col("subln"), col("subln"), 1.0 - LAMBDA_INIT, None, ALU.mult), wait=False)
        step(dve.tensor_scalar(col("qg"), col("qg"), 64.0 ** -0.5, None, ALU.mult), wait=False)
        scaled_rows("mix0", h)
        for k in range(RING):
            lo_half(k)
            if k == 1:
                turned_lo_parts("mix0", xt_lo, xt_hi)
        for t in range(T):
            dve.wait_ge(*fill(("mix0", t, 1)))
        scaled_rows("mem", mem_rows)
        dve.wait_ge(*lam_exp.at(1))
        dve.scalar_tensor_tensor(lam[:, 4:5], lam[:, 3:4], -LAMBDA_INIT, lam[:, 2:3], ALU.add, ALU.subtract)\
            .then_inc(*lam_ready.up(0))
        copy1(UNIT["l0_u"], u_nat[:, 1, :])
        for n, dst in ((0, bias1[:, 0:2, :]), (1, bias1[:, 2:4, :]), (2, bias0)):
            dve.wait_ge(*fill(("bias", n)))
            dve.tensor_copy(dst, cut(bank[:, n, :], dst.shape[1])).then_inc(freed[n], 1)
        copy1(UNIT["l0_q"], q_t[:, 2:4, :])
        turned_lo_parts("mem", mt_lo, mt_hi)
        copy1(UNIT["l0_k"], k_t[:, 2:4, :])
        for b in range(2):
            part = (slice(None), slice(2 * b, 2 * b + 2), slice(None))
            split_lo(("pool", b), part, pool_y[part])
        dve.wait_ge(*yt_ready.at(("pool", 1)))
        copy1(UNIT["l0_v"], v_nat[:, 1, :])
        dve.wait_ge(*bias_masked.at(1))
        dve.wait_ge(*lam_ready.at(0))
        for g in range(4):
            hg, qt = g // 2, g % 2
            nk = P * (qt + 1)
            e = hn[:, g % 2, :].rearrange("p (s a k) -> p s a k", s=2, a=2)
            bias = bias1 if qt else bias0
            for s in range(2):
                dve.wait_ge(*fill(("s", ("d", g), s)))
                dve.scalar_tensor_tensor(e[:, s, :, 0:nk], cut(bank[:, s, :], 2)[:, :, 0:nk], 64.0 ** -0.5,
                                         bias[:, 2 * hg:2 * hg + 2, 0:nk], ALU.mult, ALU.add)\
                    .then_inc(freed[s], 1)
            cs = slice(4 * g, 4 * g + 4)
            dve.wait_ge(*read(("s", ("d", g), 1)))
            step(dve.tensor_reduce(peak[:, cs], cut(hn[:, g % 2, :], 4)[:, :, 0:nk], AX_X, ALU.max))
            dve.tensor_scalar(shift[:, cs], peak[:, cs], -1.0, None, ALU.mult)\
                .then_inc(*shift_ready.up(("d", g)))
            u = UNIT["kv0"] + g
            lo_half(2 * u + 4)
            dve.wait_ge(*diff_exp.at(g))
            recip_total(g, 4)
            step(dve.tensor_scalar(inv[:, 4 * g + 2:4 * g + 4], inv[:, 4 * g + 2:4 * g + 4], lam[:, 4:5], None,
                                   ALU.mult), wait=False)
            for a in range(2):
                step(dve.tensor_scalar(e[:, 0, a, 0:nk], e[:, 0, a, 0:nk], inv[:, 4 * g + a:4 * g + a + 1], None,
                                       ALU.mult), wait=(a == 1))
            for a in range(2):
                ins = dve.scalar_tensor_tensor(e[:, 0, a, 0:nk], e[:, 1, a, 0:nk],
                                               inv[:, 4 * g + 2 + a:4 * g + 3 + a], e[:, 0, a, 0:nk],
                                               ALU.mult, ALU.add)
            ins.then_inc(*probs_ready.up(("d", g)))
            dve.wait_ge(half_used, 2 * u + 2)
            if g < 2:
                dve.tensor_copy(kv_k[:, 4 * g + 2:4 * g + 4, :], cut(gemm[:, 2 * (u % 2) + 1, :], 2))\
                    .then_inc(evacuated[u % 2], 1)
            else:
                dve.tensor_copy(kv_v[:, 1, (g - 2) * NB:(g - 1) * NB], gemm[:, 2 * (u % 2) + 1, :])\
                    .then_inc(evacuated[u % 2], 1)
            lo_half(2 * u + 5)
        for b in range(2):
            part = (slice(None), slice(2 * b, 2 * b + 2), slice(None))
            dve.wait_ge(*read(("h", f"d{b}", 0)))
            step(dve.reciprocal(diff_r[part], diff_r[part]))
            dve.scalar_tensor_tensor(diff_o[part], diff_o[part], col("subln"), diff_r[part], ALU.mult, ALU.mult)\
                .then_inc(*hnormed.up(f"d{b}"))
        for b in range(2):
            split_lo(("diff", b), (slice(None), slice(4 + 2 * b, 6 + 2 * b), slice(None)),
                     diff_o[:, 2 * b:2 * b + 2, :])
        add_residual(UNIT["l0_out"], 0)
        add_residual(UNIT["l0_out"] + 1, 1)

        def cross(x, filler=None):
            u = UNIT["q" + x[1]]
            for n in range(2):
                copy1(u + n, cq_t[:, 4 * n + 2:4 * n + 4, :])

            def shifts(g):
                cs = slice(4 * g, 4 * g + 2)
                dve.wait_ge(*fill(("s", (x, g), 0)))
                step(dve.tensor_reduce(peak[:, cs], cut(bank[:, g % 2, :], 2), AX_X, ALU.max))
                dve.tensor_scalar(shift[:, cs], peak[:, cs], -1.0 / 16, None, ALU.mult)\
                    .then_inc(*shift_ready.up((x, g)))

            def probs(g):
                e = cut(hn[:, g // 2, (g % 2) * NB:(g % 2 + 1) * NB], 2)
                dve.wait_ge(*read(("s", (x, g), 0)))
                recip_total(g, 2)
                for a in range(2):
                    ins = dve.tensor_scalar(e[:, a, :], e[:, a, :], inv[:, 4 * g + a:4 * g + a + 1], None,
                                            ALU.mult)
                    if a == 0:
                        step(ins, wait=False)
                ins.then_inc(*probs_ready.up((x, g)))

            shifts(0)
            shifts(1)
            probs(0)
            probs(1)
            if filler is not None:
                copy1(UNIT[filler], kv_v[:, 1, NB:D])
            for g in range(4):
                qt, hg = g // 2, g % 2
                if g + 2 < 4:
                    shifts(g + 2)
                    probs(g + 2)
                part = (slice(None), slice(4 * hg, 4 * hg + 4), slice(qt * P, (qt + 1) * P))
                dve.wait_ge(*yt_hi_ready.at((x, g)))
                dve.tensor_tensor(yt_lo[part], cut(bank[:, 3, :], 4), yt_hi[part].bitcast(F32), ALU.subtract)\
                    .then_inc(freed[3], 1)
            add_residual(UNIT["o" + x[1]], 0)
            add_residual(UNIT["o" + x[1]] + 1, 1)

        def ada_columns(m, i, a):
            dve.wait_ge(ada_landed, 16 * (8 * m + a + 1) + 32 * i)
            for n in range(ADA_COLS):
                ins = dve.tensor_tensor_reduce(ada[:, n, :], ada[:, n, :], c_act, 1.0, 0.0, ALU.mult, ALU.add,
                                               mod_part[:, ADA_COLS * a + n:ADA_COLS * a + n + 1])
            ins.then_inc(ada_used, 1)

        def mlp_chunk(m, i, last=False):
            for j in range(4):
                u = UNIT[f"mlp{m}"] + j
                if j < 2:
                    lo_half(2 * u + 4, i, last)
                    if m < 2:
                        if j == 0:
                            dve.wait_ge(ada_kept, 4 * m + 1 + i)
                        ada_columns(m, i, j)
                    r = hn[:, j, :]
                    dve.wait_ge(hid_hi[m], 2 * i + j + 1)
                    dve.tensor_tensor(r, r, r, ALU.mult).then_inc(hid_sq[m], 1)
                    dve.wait_ge(hid_sq[m], 2 * i + j + 1)
                    part = yt_lo[:, 4 * j:4 * j + 4, :]
                    dve.tensor_tensor(part, cut(r, 4), yt_hi[:, 4 * j:4 * j + 4, :].bitcast(F32), ALU.subtract)\
                        .then_inc(hid_ready[m], 1)
                    lo_half(2 * u + 5, i, last)
                else:
                    add_residual(u, j - 2, gate_f_row if m == 2 else None, i, last)
            if m < 2:
                dve.wait_ge(ada_used, 8 * m + 2 * i + 2)
                dve.tensor_copy(mod[:, bass.ds(6 * i + 24 * m, 6)], mod_part[:, :]).then_inc(ada_kept, 1)

        def mlp(m):
            if m < 2:
                with dve.Fori(0, 4) as i:
                    mlp_chunk(m, i)
            else:
                before = gate_steps[0]
                with dve.Fori(0, 3) as i:
                    mlp_chunk(m, i)
                gate_steps[0] = before
                mlp_chunk(m, 3, last=True)

        def norm(n):
            scaled_rows(n, h)
            turned_lo_parts(n, xt_lo, xt_hi)

        norm("x0")
        cross("x0")
        dve.wait_ge(*c_exp.at(0))
        step(dve.tensor_scalar(c_tmp, c_tmp, 1.0, None, ALU.add))
        step(dve.reciprocal(c_tmp, c_tmp))
        dve.tensor_tensor(c_act, c_act, c_tmp, ALU.mult).then_inc(ada_kept, 1)
        norm("mlp0")
        mlp(0)
        scaled_rows("mix1", h)
        copy1(UNIT["kv1a"], kv_k[:, 2:4, :])
        turned_lo_parts("mix1", xt_lo, xt_hi)
        step(dve.memset(z_pad[:, :, 0:2], 0.0))
        for b in range(2):
            u = UNIT["conv"] + 3 * b
            copy1(u, gate_c[:, 2:4, :])
            dve.wait_ge(*set_done(u))
            lo_half(2 * u + 6)
            for n in range(2):
                dve.wait_ge(*((bank0_done, u + 2) if n == 0 else (half_used, 2 * u + 4)))
                dve.tensor_tensor(z_pad[:, 2 * n:2 * n + 2, 2:], gate_c[:, 2 * n:2 * n + 2, :],
                                  cut(gemm[:, 2 * ((u + 1) % 2) + n, :], 2), ALU.mult)\
                    .then_inc(evacuated[(u + 1) % 2], 1)
            dve.wait_ge(*set_done(u + 1))
            dve.engine_nop().then_inc(*conv_z.up(b))
            lo_half(2 * u + 7)
            for tap in range(3):
                for c in range(4):
                    wcol = col("conv", 8 * tap + 4 * b + c)
                    z = z_pad[:, c, tap:tap + S]
                    if tap == 0:
                        ins = dve.tensor_scalar(conv_y[:, c, :], z, wcol, None, ALU.mult)
                    else:
                        ins = dve.scalar_tensor_tensor(conv_y[:, c, :], z, wcol, conv_y[:, c, :], ALU.mult,
                                                       ALU.add)
                    step(ins, wait=(c == 3))
            lo_half(2 * u + 8)
            for n in range(2):
                dve.wait_ge(*((bank0_done, u + 3) if n == 0 else (half_used, 2 * u + 6)))
                y = conv_y[:, 2 * n:2 * n + 2, :]
                dve.tensor_tensor(y, y, cut(gemm[:, 2 * (u % 2) + n, :], 2), ALU.mult)\
                    .then_inc(evacuated[u % 2], 1)
            dve.wait_ge(*set_done(u + 2))
            dve.engine_nop().then_inc(*conv_y_ready.up(b))
            split_lo(("conv", b), (slice(None), slice(4 * b, 4 * b + 4), slice(None)), conv_y)
            lo_half(2 * u + 9)
        copy1(UNIT["kv1b"], kv_k[:, 6:8, :])
        add_residual(UNIT["conv_out"], 0)
        add_residual(UNIT["conv_out"] + 1, 1)
        scaled_rows("x1", h)
        copy1(UNIT["kv1c"], kv_v[:, 1, 0:NB])
        turned_lo_parts("x1", xt_lo, xt_hi)
        cross("x1", "kv1d")
        norm("mlp1")
        mlp(1)

        dve.wait_ge(ada_kept, 9)
        dve.tensor_tensor(mod[:, :], mod[:, :], cols[:, COL["b_ada"]], ALU.add).then_inc(*mod_ready.up(0))
        for t in range(T):
            c = rstd_done.order.index(("final", t))
            dve.wait_ge(*rstd_done.at(("final", t)))
            dve.wait_ge(loaded["gain_final"], 16)
            dve.scalar_tensor_tensor(h[:, t, :], h[:, t, :], rstd[:, c:c + 1], gain, ALU.mult, ALU.mult)\
                .then_inc(*final_done.up(t))
        dve.wait_ge(*read(("row", "scale_m", 1)))
        dve.wait_ge(*read(("row", "shift_m", 1)))
        scaled_rows("mix2", h)
        dve.wait_ge(*ff_hi_ready.at(0))
        dve.tensor_tensor(ff_lo[:, :, :], ff_raw[:, :, :], ff_hi[:, :, :].bitcast(F32), ALU.subtract)\
            .then_inc(*ff_ready.up(0))
        turned_lo_parts("mix2", xt_lo, xt_hi)
        copy1(UNIT["fq"], fq_t[:, 2:4, :])
        copy1(UNIT["fk"], fk_t[:, 2:4, :])

        def head_norm(name, x, r, gains, gate=None):
            dve.wait_ge(*read(("h", name, 0)))
            dve.wait_ge(*read(("h", name, 1)))
            step(dve.reciprocal(r, r))
            if len(gains) == 1:
                ins = dve.scalar_tensor_tensor(flat(x), flat(x), gains[0], r, ALU.mult, ALU.mult)
            else:
                for c, g in enumerate(gains):
                    step(dve.scalar_tensor_tensor(x[:, c, :], x[:, c, :], g, r[:, c * S:(c + 1) * S], ALU.mult,
                                                  ALU.mult), wait=(c == 3))
                ins = dve.tensor_tensor(x, x, gate, ALU.mult)
            ins.then_inc(*hnormed.up(name))

        head_norm("fq", fq_t, hn[:, 0, :], [col("qg")])
        dve.wait_ge(*fill("ff"))
        b_forget = cols[:, COL["b_forget"]]
        step(dve.tensor_tensor(logf[:, 0, 0:8], bank[:, 2, 0:8], b_forget, ALU.add), wait=False)
        dve.tensor_tensor(logf[:, 0, 8:16], bank[:, 2, 8:16], b_forget, ALU.add).then_inc(freed[2], 1)
        dve.wait_ge(*read("ff"))
        dve.scalar_tensor_tensor(logf[:, 1, :], logf[:, 0, :], -1.0, logf[:, 0, :], ALU.mult, ALU.max)\
            .then_inc(*logf_abs.up(0))
        dve.wait_ge(*logf_ln.at(0))
        dve.scalar_tensor_tensor(logf[:, 4, :], logf[:, 0, :], 0.0, logf[:, 3, :], ALU.min, ALU.subtract)\
            .then_inc(*logf_ready.up(0))
        copy1(UNIT["fv"], fv_nat[:, 1, :])
        head_norm("fk", fk_t, hn[:, 1, :], [col("kg")])
        dve.wait_ge(*fill("cum"))
        step(dve.tensor_copy(logf[:, 5, :], bank[:, 2, 0:16]), wait=False)
        dve.tensor_scalar(cum_rows[:, :], bank[0:8, 2, P:P + S], -1.0, None, ALU.mult).then_inc(freed[2], 1)
        dve.wait_ge(*read("cum"))

        def fox_probs(g, u):
            hg, qt = g // 2, g % 2
            nk = P * (qt + 1)
            cs = slice(4 * g, 4 * g + 4)
            cum_q = logf[:, 5, 8 * qt + 4 * hg:8 * qt + 4 * hg + 4].rearrange("p (c a) -> p a c", a=2)
            dve.wait_ge(*fill(("s", ("f", g), 0)))
            dve.wait_ge(*fill(("s", ("f", g), 1)))
            both = bank[:, 0:2, :].rearrange("p n (a k) -> p (n a) k", a=2)
            step(dve.tensor_reduce(peak[:, cs], both[:, :, 0:nk], AX_X, ALU.max))
            step(dve.tensor_tensor(cut(peak[:, cs], 2), cut(peak[:, cs], 2), cum_q, ALU.add))
            dve.tensor_tensor(cut(shift[:, cs], 2), cum_q, cut(peak[:, cs], 2), ALU.subtract)\
                .then_inc(*shift_ready.up(("f", g)))
            lo_half(2 * u + 4)
            e = cut(hn[:, g % 2, :], 4)
            dve.wait_ge(*read(("s", ("f", g), 0)))
            dve.wait_ge(*read(("s", ("f", g), 1)))
            recip_total(g, 4)
            for a in range(4):
                ins = dve.tensor_scalar(e[:, a, 0:nk], e[:, a, 0:nk], inv[:, 4 * g + a:4 * g + a + 1], None,
                                        ALU.mult)
                if a < 3:
                    step(ins, wait=False)
            ins.then_inc(*probs_ready.up(("f", g)))

        def fox_unit(g, u, dst):
            fox_probs(g, u)
            dve.wait_ge(half_used, 2 * u + 2)
            src = gemm[:, 2 * (u % 2) + 1, :]
            if dst is not None:
                dve.tensor_copy(dst, cut(src, 2) if len(dst.shape) == 3 else src)\
                    .then_inc(evacuated[u % 2], 1)
            lo_half(2 * u + 5)

        def rope(name, x):
            sin = sin_m.rearrange("p (a b) -> p a b", a=1).to_broadcast((P, 2, S))
            cos = cos_m.rearrange("p (a b) -> p a b", a=1).to_broadcast((P, 4, S))
            for b in range(2):
                dve.wait_ge(*fill(("rot", name, b)))
                dve.tensor_tensor(rope_tmp[:, 2 * b:2 * b + 2, :], cut(bank[:, b, :], 2), sin, ALU.mult)\
                    .then_inc(freed[b], 1)
            step(dve.tensor_tensor(x, x, cos, ALU.mult))
            dve.wait_ge(*read(("rot", name, 0)))
            dve.wait_ge(*read(("rot", name, 1)))
            dve.tensor_tensor(x, x, rope_tmp, ALU.add).then_inc(*roped.up(name))

        fox_unit(0, UNIT["rq"], rq_t[:, 2:4, :])
        fox_unit(1, UNIT["rk"], rk_t[:, 2:4, :])
        rope("q", rq_t)
        fox_unit(2, UNIT["rv"], rv_nat[:, 1, :])
        rope("k", rk_t)
        fox_unit(3, UNIT["fog"], None)
        dve.wait_ge(*set_done(UNIT["fog"]))
        step(dve.tensor_scalar(fog_t, fog_t, 1.0, None, ALU.add))
        step(dve.reciprocal(fog_t, fog_t))
        dve.wait_ge(loaded["decay"], 16)

        def decay(a):
            dve.wait_ge(*fill(("rs", a)))
            st = hn[:, a // 2, (a % 2) * NB:(a % 2) * NB + S + P]
            step(dve.tensor_tensor(st[:, 0:S], bank[:, a % 2, 0:S], decay_m[:, a, :], ALU.mult), wait=False)
            dve.tensor_tensor(st[:, S:S + P], bank[:, a % 2, S:S + P], decay_m[:, a, 0:P], ALU.mult)\
                .then_inc(freed[a % 2], 1)
            dve.wait_ge(*read(("rs", a)))
            dve.engine_nop().then_inc(*decayed.up(a))

        decay(0)
        decay(1)
        u = UNIT["rg"]
        lo_half(2 * u + 4)
        for b in range(2):
            dve.wait_ge(*((bank0_done, u + 1) if b == 0 else (half_used, 2 * u + 2)))
            dve.tensor_copy(rg_t[:, 2 * b:2 * b + 2, :], cut(gemm[:, 2 * (u % 2) + b, :], 2))\
                .then_inc(evacuated[u % 2], 1)
        dve.wait_ge(*set_done(u))
        dve.engine_nop().then_inc(*rg_kept.up(0))
        lo_half(2 * u + 5)
        decay(2)
        decay(3)
        dve.wait_ge(*rg_exp.at(0))
        step(dve.tensor_scalar(rg_exp_t, rg_exp_t, 1.0, None, ALU.add))
        step(dve.reciprocal(rg_exp_t, rg_exp_t))
        step(dve.tensor_tensor(rg_t, rg_t, rg_exp_t, ALU.mult))
        head_norm("fo", fq_t, flat(fk_t), [col("foxg", c) for c in range(4)], fog_t)
        head_norm("ro", rq_t, flat(rk_t), [col("retg", c) for c in range(4)], rg_t)
        split_lo("fo", (slice(None), slice(0, 4), slice(None)), fq_t)
        split_lo("ro", (slice(None), slice(4, 8), slice(None)), rq_t)
        dve.wait_ge(*read(("row", "gate_m", 1)))
        add_residual(UNIT["out2"], 0, gate_m_row)
        add_residual(UNIT["out2"] + 1, 1, gate_m_row)
        dve.wait_ge(*read(("row", "scale_f", 1)))
        dve.wait_ge(*read(("row", "shift_f", 1)))
        norm("mlp2")
        dve.wait_ge(*read(("row", "gate_f", 1)))
        mlp(2)

    @block.gpsimd
    def _(gp):
        gp.memset(eps[:, :], EPS).then_inc(set_up, 1)
        gp.memset(power[:, :], -0.5).then_inc(set_up, 1)
        gp.memset(mask_bf[:, :], 0.0).then_inc(set_up, 1)
        for t in range(T):
            gp.dma_start(h[:, t, :], d["x"][t * P:(t + 1) * P, :]).then_inc(loaded["x"], 16)
        gp.dma_start(ident[:, :], d["ident"]).then_inc(loaded["consts"], 16)
        gp.dma_start(ones[:, :], d["ones"]).then_inc(loaded["consts"], 16)
        gp.dma_start(cols[:, :], d["cols"]).then_inc(loaded["consts"], 16)

        def load_gain(n):
            g = GAINS.index(n)
            gp.dma_start(gain, d["gains"][g:g + 1, :].to_broadcast((P, D))).then_inc(loaded["gain_" + n], 16)

        load_gain("mix0")
        gp.dma_start(flip_m, d["flip"]).then_inc(loaded["rel"], 16)
        gp.dma_start(bucket_m[0:BUCKETS, :], d["bucket"]).then_inc(loaded["rel"], 16)
        gp.dma_start(rel[0:BUCKETS, :], d["rel_bias"]).then_inc(loaded["rel"], 16)
        gp.dma_start(lam_in, d["lam"].to_broadcast((P, 4, 64))).then_inc(loaded["lam"], 16)
        for t in range(T):
            gp.dma_start(mem_rows[:, t, :], d["mem"][t * P:(t + 1) * P, :]).then_inc(loaded["mem"], 16)
        gp.dma_start(flat(pool_w), d["pool_w"]).then_inc(loaded["pool"], 16)
        gp.dma_start(work[:, 5120:7168], d["pool"]).then_inc(loaded["pool"], 16)
        gp.dma_start(ff_raw[:, :, :], d["ff"]).then_inc(loaded["ff"], 16)
        gp.wait_ge(set_up, 3)
        gp.affine_select(out=mask_bf[:, :], in_=mask_bf[:, :], compare_op=ALU.is_ge, fill=NEG, base=0,
                         pattern=[[-1, P]], channel_multiplier=1).then_inc(set_up, 1)
        gp.wait_ge(loaded["consts"], 48)
        gp.tensor_copy(ident_bf[:, :], ident[:, :]).then_inc(set_up, 1)

        def root(n, t):
            c = squares.order.index((n, t))
            gp.wait_ge(*squares.at((n, t)))
            gp.tensor_scalar(stat[:, c:c + 1], stat[:, c:c + 1], 1.0 / D, EPS, ALU.mult, ALU.add)\
                .then_inc(*mean_done.up((n, t)))
            gp.wait_ge(*mean_done.at((n, t)))
            gp.tensor_tensor(rstd[:, c:c + 1], stat[:, c:c + 1], power[:, :], ALU.pow)\
                .then_inc(*rstd_done.up((n, t)))

        def roots(n):
            for t in range(T):
                root(n, t)

        def next_gain(last, n):
            gp.wait_ge(*normed.at((last, T - 1)))
            load_gain(n)

        roots("mix0")
        gp.wait_ge(*read("bias_row"))
        gp.dma_start(rows_dram, bias_row[0:4, :]).then_inc(bias_stored, 16)
        next_gain("mix0", "mem")
        gp.wait_ge(bias_stored, 16)
        for dst, offset, n in ((flip1, 0, S), (flip0, P, P)):
            src = bass.AP(tensor=rows_dram.tensor, offset=offset, ap=[[1, P], [384, 4], [1, n]])
            gp.dma_start(dst, src).then_inc(loaded["flipped"], 16)
        roots("mem")
        next_gain("mem", "x0")
        gp.wait_ge(*read(("bias", 1)))
        gp.affine_select(out=bias1[:, :, P:S], in_=bias1[:, :, P:S], compare_op=ALU.is_ge, fill=NEG, base=0,
                         pattern=[[0, 4], [-1, P]], channel_multiplier=1).then_inc(*bias_masked.up(0))
        gp.wait_ge(*read(("bias", 2)))
        gp.affine_select(out=bias0, in_=bias0, compare_op=ALU.is_ge, fill=NEG, base=0,
                         pattern=[[0, 4], [-1, P]], channel_multiplier=1).then_inc(*bias_masked.up(1))
        gp.wait_ge(*read(("s", ("d", 3), 1)))
        gp.dma_start(c_act, d["c"].to_broadcast((P, D))).then_inc(loaded["c"], 16)
        roots("x0")
        next_gain("x0", "mlp0")

        def ada_loads(m):
            gp.wait_ge(*fill(("o", ("x" + str(m), 3))))
            if m == 0:
                gp.dma_start(flat(ada), d["w_ada"][0]).then_inc(ada_landed, 16)
            else:
                gp.wait_ge(ada_used, 8)
                gp.dma_start(flat(ada), d["w_ada"][8]).then_inc(ada_landed, 16)

        def more_ada(m):
            with gp.Fori(8 * m + 1, 8 * m + 8) as i:
                gp.wait_ge(ada_used, i)
                gp.dma_start(flat(ada), d["w_ada"][i]).then_inc(ada_landed, 16)

        ada_loads(0)
        roots("mlp0")
        next_gain("mlp0", "mix1")
        more_ada(0)
        roots("mix1")
        next_gain("mix1", "x1")
        roots("x1")
        next_gain("x1", "mlp1")
        ada_loads(1)
        gp.dma_start(const2, d["second"]).then_inc(loaded["const2"], 16)
        roots("mlp1")
        next_gain("mlp1", "final")
        more_ada(1)
        roots("final")
        roots("mix2")
        gp.wait_ge(*normed.at(("mix2", T - 1)))
        gp.dma_start(flat(decay_m), d["decay"]).then_inc(loaded["decay"], 16)
        roots("mlp2")


def kernel(**inputs):
    import numpy as _np
    import concourse.bacc as _bacc
    from concourse.bass_utils import run_bass_kernel_spmd as _run

    a = {k: _np.asarray(v) for k, v in inputs.items()}
    weights = {"ab_in": a["ab_w_in"][0], "conv_in": a["conv_w_in"][0], "conv_out": a["conv_w_out"][0],
               "out2": a["w_out_2"][0], "w1_2": a["w_mlp_in_2"][0], "w2_2": a["w_mlp_out_2"][0]}
    weights["ab_out"] = _np.concatenate([a["ab_w_out"][0][512:], a["ab_w_out"][0][:512]])
    for l in range(2):
        weights[f"wkv{l}"], weights[f"wq{l}"], weights[f"wo{l}"] = (
            a["xattn_wkv"][l], a["xattn_wq"][l], a["xattn_wo"][l])
        weights[f"w1_{l}"], weights[f"w2_{l}"] = a["mlp_w1"][l], a["mlp_w2"][l]
    w_in = a["w_in_2"][0]
    weights["in2"] = _np.concatenate([w_in[:, :2048], w_in[:, 2056:]], axis=1)
    stream = _np.stack([weights[n][D * r:D * (r + 1), NB * c:NB * (c + 1)] for n, r, c in UNITS])
    stream = stream.reshape(NH, HC, P, NB).transpose(0, 2, 1, 3)
    columns = [a["subln_g"][0][:, None], a["pool_scale"][0].reshape(4, P).T,
               a["conv_w"][0].reshape(24, P).T,
               _np.tile(a["q_norm_gain_2"][0], 2)[:, None], _np.tile(a["k_norm_gain_2"][0], 2)[:, None],
               a["fox_out_gain_2"][0].reshape(4, P).T, a["ret_out_gain_2"][0].T,
               a["b_ada_2"][0].reshape(48, P).T, _np.broadcast_to(a["b_forget_2"], (P, 8))]
    gains = {"mix0": a["norm_mix_g"][0], "mem": a["mem_norm_g"], "x0": a["norm_xattn_g"][0],
             "mlp0": a["norm_mlp_g"][0], "mix1": a["norm_mix_g"][1], "x1": a["norm_xattn_g"][1],
             "mlp1": a["norm_mlp_g"][1], "final": a["final_norm_g"]}
    arrays = {
        "weights": stream,
        "x": a["x"][0], "mem": a["mem"][0],
        "cols": _np.concatenate(columns, axis=1),
        "gains": _np.stack([gains[n] for n in GAINS]),
        "rel_bias": a["rel_bias"],
        "lam": _np.stack([a["lambda_q1"], a["lambda_k1"], a["lambda_q2"], a["lambda_k2"]], axis=1),
        "pool_w": a["pool_w"][0].transpose(1, 0, 2).reshape(P, -1),
        "ff": w_in[:, 2048:2056].reshape(KC, P, 8).transpose(1, 0, 2),
        "c": a["c_2"],
        "w_ada": a["w_ada_2"][0].T.reshape(ADA_LOADS, ADA_COLS, P, D).transpose(0, 2, 1, 3)
                 .reshape(ADA_LOADS, P, ADA_COLS * D),
    }
    arrays.update(constants())
    arrays = {k: _np.ascontiguousarray(v) for k, v in arrays.items()}
    nc = _bacc.Bacc("TRN2", target_bir_lowering=False, num_devices=1)
    d = {k: nc.dram_tensor("in_" + k, v.shape, mybir.dt.from_np(v.dtype), kind="ExternalInput").ap()
         for k, v in arrays.items()}
    out = nc.dram_tensor("out_y", (S, D), F32, kind="ExternalOutput").ap()
    build(nc, d, out)
    r = _run(nc, [{"in_" + k: v for k, v in arrays.items()}], core_ids=[0])
    return r.results[0]["out_y"].reshape(1, S, D)
```

```python
from contextlib import ExitStack
import math

import numpy as np

import concourse.bass as bass
from concourse import mybir

F32 = mybir.dt.float32
F32R = mybir.dt.float32r
BF16 = mybir.dt.bfloat16
ALU = mybir.AluOpType
ACT = mybir.ActivationFunctionType
AX_X = mybir.AxisListType.X

P = 128
D = 1024
S = 256
T = S // P
KC = D // P
NB = 512
HC = KC // 2
HALF = HC * NB
RING = 4
EPS = 1e-6
NEG = -1e30
LAMBDA_INIT = 0.8 - 0.6 * math.exp(-0.3 * 0)
BUCKETS, MAX_EXACT, MAX_DIST = 32, 16, 128
WINDOWS = (2, 4, 8, 16)
ADA_COLS = 3
ADA_LOADS = 16

def _blocks(name, cols, row=0):
    return [(name, row, c) for c in cols]


def _mlp(w1, w2):
    out = []
    for j in range(4):
        out += _blocks(w1, (2 * j, 2 * j + 1)) + _blocks(w2, (0, 1), j)
    return out


SECTIONS = [
    ("l0_u", _blocks("ab_in", [3])),
    ("l0_q", _blocks("ab_in", [0])),
    ("l0_k", _blocks("ab_in", [1])),
    ("l0_v", _blocks("ab_in", [2])),
    ("kv0", _blocks("wkv0", [0, 1, 2, 3])),
    ("l0_out", _blocks("ab_out", [0, 1])),
    ("q0", _blocks("wq0", [0, 1])),
    ("o0", _blocks("wo0", [0, 1])),
    ("kv1b", _blocks("wkv1", [1])),
    ("mlp0", _mlp("w1_0", "w2_0")),
    ("kv1a", _blocks("wkv1", [0])),
    ("conv", _blocks("conv_in", [2, 4, 0, 3, 5, 1])),
    ("conv_out", _blocks("conv_out", [0, 1])),
    ("kv1c", _blocks("wkv1", [2])),
    ("q1", _blocks("wq1", [0, 1])),
    ("kv1d", _blocks("wkv1", [3])),
    ("o1", _blocks("wo1", [0, 1])),
    ("mlp1", _mlp("w1_1", "w2_1")),
    ("fq", _blocks("in2", [0])),
    ("fk", _blocks("in2", [1])),
    ("fv", _blocks("in2", [2])),
    ("rq", _blocks("in2", [4])),
    ("rk", _blocks("in2", [5])),
    ("rv", _blocks("in2", [6])),
    ("fog", _blocks("in2", [3])),
    ("rg", _blocks("in2", [7])),
    ("out2", _blocks("out2", [0, 1])),
    ("mlp2", _mlp("w1_2", "w2_2")),
]
UNIT = {}
UNITS = []
for _name, _list in SECTIONS:
    UNIT[_name] = len(UNITS)
    UNITS += _list
NU = len(UNITS)
NH = 2 * NU

NORMS = ["mix0", "mem", "x0", "mlp0", "mix1", "x1", "mlp1", "mix2", "mlp2"]
STATS = NORMS[:7] + ["final"] + NORMS[7:]
GAINS = ["mix0", "mem", "x0", "mlp0", "mix1", "x1", "mlp1", "final"]


class Signal:

    def __init__(self, sem, labels):
        self.sem = sem
        self.order = list(labels)
        self.value = {label: n + 1 for n, label in enumerate(self.order)}
        self.raised = 0

    def at(self, label):
        return self.sem, self.value[label]

    def up(self, label):
        assert self.order[self.raised] == label, (self.order[self.raised], label)
        self.raised += 1
        return self.sem, 1


def constants():
    f = np.float32
    c = {}
    c["ident"] = np.eye(P, dtype=f)
    c["ones"] = np.ones((P, P), f)
    c["flip"] = np.eye(P, dtype=f)[::-1].copy()
    dist = np.maximum(S - 1 - np.arange(384), 0)
    nf = np.maximum(dist, 1).astype(f)
    large = MAX_EXACT + (np.log(nf / f(MAX_EXACT)) / f(math.log(MAX_DIST / MAX_EXACT))
                         * f(BUCKETS - MAX_EXACT)).astype(np.int32)
    bucket = np.where(dist < MAX_EXACT, dist, np.minimum(large, BUCKETS - 1))
    c["bucket"] = (np.arange(BUCKETS)[:, None] == bucket[None, :]).astype(f)
    t = np.arange(S)
    pool = np.zeros((S, len(WINDOWS), S), f)
    for g, w in enumerate(WINDOWS):
        inside = (t[None, :] >= t[:, None]) & (t[None, :] - t[:, None] < w)
        pool[:, g, :] = inside / np.minimum(t + 1, w).astype(f)[None, :] - np.eye(S, dtype=f)
    c["pool"] = pool.reshape(T, P, len(WINDOWS), S).transpose(1, 0, 2, 3).reshape(P, -1)
    rot = np.zeros((P, P), f)
    for d in range(64):
        rot[d + 64, d] = -1.0
        rot[d, d + 64] = 1.0
    tri = (np.arange(P)[:, None] <= np.arange(P)[None, :]).astype(f)
    freq = f(10000.0) ** (-np.arange(0, P, 2, dtype=f) / f(P))
    ang = (np.arange(S, dtype=f)[None, :] * np.concatenate([freq, freq])[:, None]).astype(f)
    c["second"] = np.concatenate([rot, tri, np.cos(ang), np.sin(ang)], axis=1).astype(f)
    log_g = np.log(1.0 - 2.0 ** (-5.0 - np.arange(4, dtype=np.float64)))
    diff = np.arange(S)[None, :] - np.arange(P)[:, None]
    decay = np.where(diff[:, None, :] >= 0,
                     np.exp(np.maximum(diff, 0)[:, None, :] * log_g[None, :, None]), 0.0)
    c["decay"] = (decay * 128.0 ** -0.5).astype(f).reshape(P, -1)
    return {k: np.ascontiguousarray(v, dtype=f) for k, v in c.items()}


COL = {}
_at = 0
for _name, _n in (("subln", 1), ("pool_scale", 4), ("conv", 24), ("qg", 1), ("kg", 1), ("foxg", 4),
                  ("retg", 4), ("b_ada", 48), ("b_forget", 8), ("halves", 2)):
    COL[_name] = slice(_at, _at + _n)
    _at += _n
N_COLS = _at


def build(nc, d, out):
    ctx = ExitStack()
    with ctx:
        program(nc, ctx, d, out)


def program(nc, ctx, d, out):
    def sb(name, shape, dt=F32):
        return ctx.enter_context(nc.sbuf_tensor(name, shape, dt))

    def sem(name):
        return ctx.enter_context(nc.semaphore(name))

    def signal(name, labels):
        return Signal(sem(name), labels)

    raw = sb("raw", [P, RING, HC, NB])
    hi = sb("hi", [P, RING, HC, NB], F32R)
    lo = sb("lo", [P, RING, HC, NB], F32R)
    xt_hi = sb("xt_hi", [P, KC, S], F32R)
    xt_lo = sb("xt_lo", [P, KC, S], F32R)
    yt_hi = sb("yt_hi", [P, KC, S], F32R)
    yt_lo = sb("yt_lo", [P, KC, S], F32R)
    mt_hi = sb("mt_hi", [P, KC, S], F32R)
    mt_lo = sb("mt_lo", [P, KC, S], F32R)
    h = sb("h", [P, T, D])
    hn = sb("hn", [P, T, D])
    work = sb("work", [P, 11264])
    ident = sb("ident", [P, P])
    ones = sb("ones", [P, P])
    cols = sb("cols", [P, N_COLS])
    mod = sb("mod", [P, 48])
    mod_part = sb("mod_part", [P, 2 * ADA_COLS])
    stat = sb("stat", [P, 2 * len(STATS)])
    rstd = sb("rstd", [P, 2 * len(STATS)])
    power = sb("power", [P, 1])
    eps = sb("eps", [P, 1])
    peak = sb("peak", [P, 16])
    shift = sb("shift", [P, 16])
    total = sb("total", [P, 16])
    inv = sb("inv", [P, 16])
    head_inv = sb("head_inv", [P, 16])
    lam = sb("lam", [P, 8])
    mask_bf = sb("mask_bf", [P, P], BF16)
    ident_bf = sb("ident_bf", [P, P], BF16)
    ff_raw = sb("ff_raw", [P, KC, 8])
    ff_hi = sb("ff_hi", [P, KC, 8], F32R)
    ff_lo = sb("ff_lo", [P, KC, 8], F32R)
    logf = sb("logf", [P, 6, 2 * 8])
    gemm = ctx.enter_context(nc.psum_tensor("gemm", [P, 4, NB], F32))
    bank = ctx.enter_context(nc.psum_tensor("bank", [P, 4, NB], F32))

    def w(start, *shape):
        n = int(np.prod(shape))
        flat = work[:, start:start + n]
        if len(shape) == 2:
            return flat.rearrange("p (a b) -> p a b", a=shape[0])
        if len(shape) == 3:
            return flat.rearrange("p (a b c) -> p a b c", a=shape[0], b=shape[1])
        return flat

    def cut(ap, a):
        return ap.rearrange("p (a b) -> p a b", a=a)

    def flat(ap):
        return ap.rearrange("p a b -> p (a b)")

    def col(name, n=0):
        return cols[:, COL[name].start + n:COL[name].start + n + 1]

    q_t, k_t, v_nat = w(0, 4, S), w(1024, 4, S), w(2048, T, NB)
    bias1, bias0 = w(3072, 4, S), w(4096, 4, P)
    flip1, flip0 = w(0, 4, S), w(1024, 4, P)
    kv_k, kv_v = w(5120, KC, S), w(7168, T, D)
    mem_rows = w(7168, T, D)
    u_nat, pool_y, lam_in = w(2048, T, NB), w(2048, 4, S), w(2048, 4, 64)
    pool_w, pool_m = w(4608, 4, P), w(5120, T, 4, S)
    gain = w(9216, D)
    pool_t, a_t = w(10240, 4, S), w(10240, 2, 4, P)
    flip_m, bucket_m, rel, bias_row = w(10240, P), w(10368, 384), w(10752, 4), w(10756, 384)
    diff_o, diff_sq = w(0, 4, S), w(1024, 4, S)
    cq_t, p_t = w(0, KC, S), w(2048, 2, 4, P)
    ada, c_tmp, c_act = w(0, ADA_COLS, D), w(3072, D), w(4096, D)
    gate_c, z_pad, conv_y = w(0, 4, S), w(1024, 4, S + 2), w(2056, 4, S)
    fq_t, fk_t, fv_nat, fog_t = w(0, 4, S), w(1024, 4, S), w(2048, T, NB), w(3072, 4, S)
    rq_t, rk_t, rv_nat, rg_t = w(4096, 4, S), w(5120, 4, S), w(6144, T, NB), w(7168, 4, S)
    rg_exp_t, rope_tmp = w(2048, 4, S), w(7168, 4, S)
    const2 = w(8192, 768)
    rot_m, tri_m = const2[:, 0:128], const2[:, 128:256]
    cos_m, sin_m = const2[:, 256:512], const2[:, 512:768]
    cum_rows = w(3072, S)[0:8]
    decay_m, shift_row, e_t = w(9216, 4, S), w(10240, D), w(10240, 8, P)
    scale_row = w(5120, D)
    gate_m_row, gate_f_row, gated = w(1024, D), w(3072, D), w(5120, T, NB)

    rows_dram = nc.dram_tensor("bias_rows", (4, 384), F32, kind="Internal").ap()

    landed = [sem(f"half_landed{n}") for n in range(RING)]
    hi_ready, lo_ready = sem("hi_ready"), sem("lo_ready")
    half_used = sem("half_used")
    bank0_done = sem("bank0_done")
    evacuated = [sem(f"set_evacuated{n}") for n in range(2)]
    filled = [sem(f"bank_filled{n}") for n in range(4)]
    freed = [sem(f"bank_freed{n}") for n in range(4)]
    hid_hi = [sem(f"hidden_hi{m}") for m in range(3)]
    hid_sq = [sem(f"hidden_square{m}") for m in range(3)]
    hid_ready = [sem(f"hidden_ready{m}") for m in range(3)]
    gated_done = sem("gated_done")
    ada_landed, ada_used, ada_kept = sem("ada_landed"), sem("ada_used"), sem("ada_kept")
    loads = (["x", "ident", "mem", "consts", "rel", "lam", "pool", "flipped", "c", "ff", "const2", "decay"]
             + ["gain_" + g for g in GAINS])
    loaded = {name: sem("loaded_" + name) for name in loads}
    bias_stored, out_stored = sem("bias_stored"), sem("out_stored")

    stat_tiles = [(n, t) for n in STATS for t in range(T)]
    norm_tiles = [(n, t) for n in NORMS for t in range(T)]
    squares = signal("squares_summed", stat_tiles)
    mean_done = signal("mean_done", stat_tiles)
    rstd_done = signal("rstd_done", stat_tiles)
    final_done = signal("final_norm_done", range(T))
    normed = signal("normed", norm_tiles)
    turned_hi = signal("transposed_hi", [(n, t, j) for n, t in norm_tiles for j in range(2)])
    vec_step, act_step = sem("vector_step"), sem("scalar_step")
    set_up = sem("constants_set")
    bias_masked = signal("bias_masked", [0, 1])
    pool_y_ready = signal("pool_y_ready", [0, 1])
    YT = [("pool", 0), ("pool", 1), ("diff", 0), ("diff", 1), ("conv", 0), ("conv", 1), "fo", "ro"]
    yt_ready = signal("yt_ready", YT)
    yt_hi_ready = signal("yt_hi_ready", YT[0:4] + [("x0", g) for g in range(4)] + YT[4:6]
                         + [("x1", g) for g in range(4)] + YT[6:8])
    lam_sums, lam_exp, lam_ready = (signal("lambda_sums", [0, 1]), signal("lambda_exp", [0, 1]),
                                    signal("lambda_ready", [0]))
    GROUPS = [(name, g) for name in ("d", "x0", "x1", "f") for g in range(4)]
    shift_ready = signal("shift_ready", GROUPS)
    diff_exp = signal("diff_exp", range(4))
    probs_ready = signal("probs_ready", GROUPS)
    HEADS = ["d", "fq", "fk", "fo", "ro"]
    hsq = signal("head_squares", HEADS)
    hnormed = signal("head_normed", HEADS)
    hinverse = signal("head_inverse", HEADS)
    c_exp = signal("c_exp", [0])
    mod_ready = signal("mod_ready", [0, 1])
    conv_z, conv_y_ready = signal("conv_z", [0, 1]), signal("conv_y", [0, 1])
    ff_hi_ready, ff_ready = signal("ff_hi", [0]), signal("ff_ready", [0])
    logf_abs, logf_ln, logf_ready = (signal("logf_abs", [0]), signal("logf_ln", [0]),
                                     signal("logf_ready", [0]))
    roped = signal("roped", ["q", "k"])
    decayed = signal("decayed", range(4))
    rg_kept, rg_exp = signal("rg_kept", [0]), signal("rg_exp", [0])

    fills = {}
    bank_uses = [0, 0, 0, 0]

    def fill(label):
        n, k = fills[label]
        return filled[n], k

    def read(label):
        n, k = fills[label]
        return freed[n], k

    def turn_bank(t, j):
        return 2 * (T - 1 - t) + j

    def set_done(u, tiles=2):
        return evacuated[u % 2], 2 * (u // 2) + tiles

    block = ctx.enter_context(nc.Block())

    @block.sync
    def _(sp):
        for t in range(T):
            sp.dma_start(h[:, t, :], d["x"][t * P:(t + 1) * P, :]).then_inc(loaded["x"], 16)
        for s in range(RING):
            sp.dma_start(raw[:, s], d["weights"][s]).then_inc(landed[s], 16)
        with sp.Fori(1, NH // RING) as i:
            for s in range(RING):
                sp.wait_ge(lo_ready, RING * i + (s - RING + 1))
                sp.dma_start(raw[:, s], d["weights"][RING * i + s]).then_inc(landed[s], 16)
        for t in range(T):
            sp.wait_ge(*set_done(NU - 1, t + 1))
            sp.dma_start(out[t * P:(t + 1) * P, :], h[:, t, :]).then_inc(out_stored, 16)
        sp.wait_ge(out_stored, 16 * T)

    @block.tensor
    def _(pe):
        XT, YT_, MT = (xt_hi, xt_lo), (yt_hi, yt_lo), (mt_hi, mt_lo)

        def claim(n, label):
            if bank_uses[n]:
                pe.wait_ge(freed[n], bank_uses[n])
            bank_uses[n] += 1
            fills[label] = (n, bank_uses[n])

        def unit(u, x, stationary, waits=(None, None), i=None, mid=None):
            s = u % 2
            if u >= 2:
                pe.wait_ge(evacuated[s], 2 * (u // 2) + (0 if i is None else 4 * i))
            for b in range(2):
                if b == 1 and mid is not None:
                    mid()
                slot = (2 * u + b) % RING
                pe.wait_ge(lo_ready, 2 * u + b + 1 + (0 if i is None else 8 * i))
                if waits[b] is not None:
                    pe.wait_ge(*waits[b])
                pairs = ((x[0], hi), (x[0], lo), (x[1], hi))
                if stationary == "x":
                    for t in range(T):
                        for k in range(HC):
                            c = b * HC + k
                            for n, (xs, ws) in enumerate(pairs):
                                mm = pe.matmul(gemm[:, 2 * s + t, :], xs[:, c, t * P:(t + 1) * P],
                                               ws[:, slot, k, :], start=(c == 0 and n == 0),
                                               stop=(c == KC - 1 and n == 2), skip_group_check=True)
                        if b == 1 and t == 0:
                            mm.then_inc(bank0_done, 1)
                else:
                    for j in range(4):
                        o = gemm[:, 2 * s + j // 2, (j % 2) * S:(j % 2 + 1) * S]
                        for k in range(HC):
                            c = b * HC + k
                            for n, (xs, ws) in enumerate(pairs):
                                mm = pe.matmul(o, ws[:, slot, k, j * P:(j + 1) * P], xs[:, c, :],
                                               start=(c == 0 and n == 0 and j % 2 == 0),
                                               stop=(c == KC - 1 and n == 2), skip_group_check=True)
                        if b == 1 and j == 1:
                            mm.then_inc(bank0_done, 1)
                mm.then_inc(half_used, 1)

        def transposes(n):
            for t in range(T):
                pe.wait_ge(*normed.at((n, t)))
                for j in range(2):
                    b = turn_bank(t, j)
                    claim(b, (n, t, j))
                    for k in range(HC):
                        c = j * HC + k
                        mm = pe.transpose(bank[:, b, k * P:(k + 1) * P],
                                          hn[:, t, c * P:(c + 1) * P], ident[:, :])
                    mm.then_inc(filled[b], 1)

        def split(n):
            return read((n, T - 1, 0)), read((n, T - 1, 1))

        def turn_probs(grp, e, heads, tiles, part=0):
            claim(2, ("t", grp, part))
            for n, (a, b) in enumerate([(a, b) for a in heads for b in tiles]):
                mm = pe.transpose(bank[:, 2, n * P:(n + 1) * P], e[:, a, b * P:(b + 1) * P], ident[:, :])
            mm.then_inc(filled[2], 1)

        col_halves = cols[:, COL["halves"]]

        def head_sums(name, halves, sq):
            pe.wait_ge(*hsq.at(name))
            claim(0, ("h", name))
            n = halves.shape[1]
            for t in range(T):
                for c in range(4):
                    mm = pe.matmul(bank[:, 0, (4 * t + c) * n:(4 * t + c + 1) * n],
                                   sq[:, c, t * P:(t + 1) * P], halves, start=True, stop=True,
                                   skip_group_check=True)
            mm.then_inc(filled[0], 1)

        def head_back(name, wide=None):
            pe.wait_ge(*hinverse.at(name))
            for b in range(2):
                claim(b, ("b", name, b))
                for c in (2 * b, 2 * b + 1):
                    for t in range(T):
                        m = 4 * t + c
                        r = (head_inv[:, m:m + 1].to_broadcast((P, P)) if wide is None
                             else wide[:, m * P:(m + 1) * P])
                        mm = pe.matmul(bank[:, b, (c % 2) * S + t * P:(c % 2) * S + (t + 1) * P],
                                       r, ident[:, :], start=True, stop=True, skip_group_check=True)
                mm.then_inc(filled[b], 1)

        def row(name, index, first):
            for j in range(2):
                claim(first + j, ("row", name, j))
                for k in range(HC):
                    m = index * KC + j * HC + k
                    mm = pe.matmul(bank[:, first + j, k * P:(k + 1) * P],
                                   mod[:, m:m + 1].to_broadcast((P, P)), ident[:, :],
                                   start=True, stop=True, skip_group_check=True)
                mm.then_inc(filled[first + j], 1)

        def out_units(name, w0, w1, mids=(None, None)):
            unit(UNIT[name], YT_, "x", (w0, w1), mid=mids[0])
            unit(UNIT[name] + 1, YT_, "x", mid=mids[1])

        def bias_rows():
            pe.wait_ge(loaded["rel"], 48)
            claim(0, "bias_row")
            pe.matmul(bank[0:4, 0, 0:384], rel[0:BUCKETS, :], bucket_m[0:BUCKETS, :], start=True, stop=True)\
                .then_inc(filled[0], 1)

        def bias_turned():
            pe.wait_ge(loaded["flipped"], 32)
            for n, src in ((0, flip1[:, 0:2, :]), (1, flip1[:, 2:4, :]), (2, flip0)):
                claim(n, ("bias", n))
                pe.matmul(bank[:, n, :], flip_m, flat(src), start=True, stop=True).then_inc(filled[n], 1)

        bias_rows()
        pe.wait_ge(loaded["ident"], 16)
        transposes("mix0")
        unit(UNIT["l0_u"], XT, "x", split("mix0"))
        unit(UNIT["l0_q"], XT, "w", mid=bias_turned)
        pe.wait_ge(loaded["pool"], 32)
        pe.wait_ge(*set_done(UNIT["l0_u"]))
        for g in range(4):
            n = g // 2
            if g % 2 == 0:
                claim(n, ("pool_t", n))
            for t in range(T):
                mm = pe.matmul(bank[:, n, (g % 2) * S:(g % 2 + 1) * S], u_nat[:, t, g * P:(g + 1) * P],
                               pool_m[:, t, g, :], start=(t == 0), stop=(t == T - 1), skip_group_check=True)
            if g % 2 == 1:
                mm.then_inc(filled[n], 1)
        unit(UNIT["l0_k"], XT, "w", mid=lambda: transposes("mem"))
        for g in range(4):
            n = g // 2
            if g % 2 == 0:
                pe.wait_ge(*read(("pool_t", n)))
                claim(2 + n, ("pool_y", n))
            mm = pe.matmul(bank[:, 2 + n, (g % 2) * S:(g % 2 + 1) * S], pool_w[:, g, :], pool_t[:, g, :],
                           start=True, stop=True, skip_group_check=True)
            if g % 2 == 1:
                mm.then_inc(filled[2 + n], 1)
        unit(UNIT["l0_v"], XT, "x")

        pe.wait_ge(*set_done(UNIT["l0_q"]))
        pe.wait_ge(*set_done(UNIT["l0_k"]))
        for g in range(4):
            hg, qt = g // 2, g % 2
            nk = P * (qt + 1)
            for s in range(2):
                claim(s, ("s", ("d", g), s))
                r = slice(64 * s, 64 * s + 64)
                for a in range(2):
                    mm = pe.matmul(bank[:, s, a * S:a * S + nk], q_t[r, 2 * hg + a, qt * P:(qt + 1) * P],
                                   k_t[r, 2 * hg + a, 0:nk], start=True, stop=True, skip_group_check=True)
                mm.then_inc(filled[s], 1)
            unit(UNIT["kv0"] + g, MT, "w" if g < 2 else "x", split("mem") if g == 0 else (None, None))
            if g == 0:
                pe.wait_ge(*set_done(UNIT["l0_v"]))
            pe.wait_ge(*probs_ready.at(("d", g)))
            turn_probs(("d", g), cut(hn[:, g % 2, 0:2 * S], 2), range(2), range(qt + 1))
            pe.wait_ge(*read(("t", ("d", g), 0)))
            if qt == 0:
                claim(3, ("o", ("d", hg)))
            for a in range(2):
                for kt in range(qt + 1):
                    mm = pe.matmul(bank[:, 3, a * S + qt * P:a * S + (qt + 1) * P],
                                   v_nat[:, kt, (2 * hg + a) * P:(2 * hg + a + 1) * P],
                                   a_t[:, g % 2, a * (qt + 1) + kt, :],
                                   start=(kt == 0), stop=(kt == qt), skip_group_check=True)
            if qt == 1:
                mm.then_inc(filled[3], 1)
        head_sums("d", ones[:, 0:1], diff_sq)
        head_back("d")
        out_units("l0_out", yt_ready.at(("pool", 1)), yt_ready.at(("diff", 1)))

        def cross(x, filler=None, mids=(None, None)):
            u = UNIT["q" + x[1]]

            def scores(g):
                hg, qt = g // 2, g % 2
                pe.wait_ge(*set_done(u + hg))
                claim(g % 2, ("s", (x, g), 0))
                for a in range(2):
                    for dc in range(2):
                        c = (2 * hg + a) * 2 + dc
                        mm = pe.matmul(bank[:, g % 2, a * S:(a + 1) * S], cq_t[:, c, qt * P:(qt + 1) * P],
                                       kv_k[:, c, :], start=(dc == 0), stop=(dc == 1), skip_group_check=True)
                mm.then_inc(filled[g % 2], 1)

            def first_scores():
                scores(0)
                scores(1)

            unit(u, XT, "w", split(x))
            unit(u + 1, XT, "w", mid=first_scores)
            if filler is not None:
                unit(UNIT[filler], MT, "x")
                pe.wait_ge(*set_done(UNIT[filler]))
            for g in range(4):
                hg = g // 2
                pe.wait_ge(*probs_ready.at((x, g)))
                turn_probs((x, g), cut(hn[:, g // 2, (g % 2) * NB:(g % 2 + 1) * NB], 2), range(2), range(2))
                if g + 2 < 4:
                    scores(g + 2)
                pe.wait_ge(*read(("t", (x, g), 0)))
                claim(3, ("o", (x, g)))
                for a in range(2):
                    for dc in range(2):
                        c = (2 * hg + a) * 2 + dc
                        for mt in range(2):
                            mm = pe.matmul(bank[:, 3, (2 * a + dc) * P:(2 * a + dc + 1) * P],
                                           kv_v[:, mt, c * P:(c + 1) * P], p_t[:, g % 2, 2 * a + mt, :],
                                           start=(mt == 0), stop=(mt == 1), skip_group_check=True)
                mm.then_inc(filled[3], 1)
            out_units("o" + x[1], read(("o", (x, 1))), read(("o", (x, 3))), mids)

        def mlp(m, n):
            u0 = UNIT[f"mlp{m}"]
            with pe.Fori(0, 4) as i:
                unit(u0, XT, "w", split(n), i=i)
                unit(u0 + 1, XT, "w", i=i)
                unit(u0 + 2, YT_, "x", ((hid_ready[m], 2 * i + 1), (hid_ready[m], 2 * i + 2)), i=i)
                unit(u0 + 3, YT_, "x", i=i)

        transposes("x0")
        cross("x0")
        unit(UNIT["kv1b"], MT, "w", mid=lambda: transposes("mlp0"))
        mlp(0, "mlp0")
        unit(UNIT["kv1a"], MT, "w", mid=lambda: transposes("mix1"))
        for n in range(6):
            unit(UNIT["conv"] + n, XT, "w", split("mix1") if n == 0 else (None, None))
        out_units("conv_out", yt_ready.at(("conv", 0)), yt_ready.at(("conv", 1)))
        unit(UNIT["kv1c"], MT, "x", mid=lambda: transposes("x1"))

        def shift_m():
            pe.wait_ge(*mod_ready.at(0))
            row("shift_m", 0, 0)

        cross("x1", "kv1d", (shift_m, lambda: row("scale_m", 1, 2)))
        transposes("mlp1")
        mlp(1, "mlp1")

        transposes("mix2")
        unit(UNIT["fq"], XT, "w", split("mix2"))
        unit(UNIT["fk"], XT, "w", mid=lambda: head_sums("fq", col_halves, cut(hn[:, 0, :], 4)))
        head_back("fq", hn[:, 0, :])
        pe.wait_ge(*ff_ready.at(0))
        claim(2, "ff")
        for t in range(T):
            for c in range(KC):
                for n, (xs, ws) in enumerate(((xt_hi, ff_hi), (xt_hi, ff_lo), (xt_lo, ff_hi))):
                    mm = pe.matmul(bank[:, 2, t * 8:(t + 1) * 8], xs[:, c, t * P:(t + 1) * P], ws[:, c, :],
                                   start=(c == 0 and n == 0), stop=(c == KC - 1 and n == 2),
                                   skip_group_check=True)
        mm.then_inc(filled[2], 1)

        def fox_gates():
            head_sums("fk", col_halves, cut(hn[:, 1, :], 4))
            pe.wait_ge(loaded["const2"], 16)
            pe.wait_ge(*logf_ready.at(0))
            claim(2, "cum")
            lf0, lf1 = logf[:, 4, 0:8], logf[:, 4, 8:16]
            for o, terms in ((bank[:, 2, 0:8], [(tri_m, lf0)]),
                             (bank[:, 2, 8:16], [(ones[:, :], lf0), (tri_m, lf1)]),
                             (bank[0:8, 2, 128:256], [(lf0, tri_m)]),
                             (bank[0:8, 2, 256:384], [(lf0, ones[:, :]), (lf1, tri_m)])):
                for n, (a, b) in enumerate(terms):
                    mm = pe.matmul(o, a, b, start=(n == 0), stop=(n == len(terms) - 1), skip_group_check=True)
            mm.then_inc(filled[2], 1)
            head_back("fk", hn[:, 1, :])

        unit(UNIT["fv"], XT, "x", mid=fox_gates)

        def fox_scores(g):
            hg, qt = g // 2, g % 2
            nk = P * (qt + 1)
            for b in range(2):
                claim(b, ("s", ("f", g), b))
                r = slice(64 * b, 64 * b + 64)
                for a in range(2):
                    c = 2 * hg + a
                    o = bank[:, b, a * S:a * S + nk]
                    pe.matmul(o, fq_t[r, c, qt * P:(qt + 1) * P], fk_t[r, c, 0:nk], start=True, stop=False,
                              skip_group_check=True)
                    pe.matmul(o, ident[0:8, 2 * c + b:2 * c + b + 1].to_broadcast((8, P)), cum_rows[:, 0:nk],
                              start=False, stop=False, skip_group_check=True)
                    mm = pe.matmul(bank[:, b, a * S + qt * P:a * S + (qt + 1) * P], ident_bf[:, :],
                                   mask_bf[:, :], start=False, stop=True, skip_group_check=True)
                mm.then_inc(filled[b], 1)

        def fox_values(g):
            hg, qt = g // 2, g % 2
            e = cut(hn[:, g % 2, :], 4)
            pe.wait_ge(*probs_ready.at(("f", g)))
            for part in range(qt + 1):
                turn_probs(("f", g), e, range(4) if qt == 0 else range(2 * part, 2 * part + 2),
                           range(qt + 1), part)
            if qt == 0:
                claim(3, ("o", ("f", hg)))
            for a in range(4):
                if a == 0 or (a == 2 and qt == 1):
                    pe.wait_ge(*read(("t", ("f", g), a // 2)))
                r = slice(64 * (a // 2), 64 * (a // 2) + 64)
                hd = 4 * hg + 2 * (a % 2) + a // 2
                for kt in range(qt + 1):
                    mm = pe.matmul(bank[r, 3, (a % 2) * S + qt * P:(a % 2) * S + (qt + 1) * P],
                                   fv_nat[:, kt, hd * 64:(hd + 1) * 64], e_t[:, a * (qt + 1) + kt, :],
                                   start=(kt == 0), stop=(kt == qt), skip_group_check=True)
            if qt == 1:
                mm.then_inc(filled[3], 1)

        def rotated(name, src, u):
            pe.wait_ge(*set_done(UNIT[u]))
            for b in range(2):
                claim(b, ("rot", name, b))
                pe.matmul(bank[:, b, :], rot_m, flat(src[:, 2 * b:2 * b + 2, :]), start=True, stop=True)\
                    .then_inc(filled[b], 1)

        pe.wait_ge(*hnormed.at("fk"))
        pe.wait_ge(*read("cum"))
        fox_scores(0)
        unit(UNIT["rq"], XT, "w")
        pe.wait_ge(*set_done(UNIT["fv"]))
        fox_values(0)
        fox_scores(1)
        unit(UNIT["rk"], XT, "w")
        fox_values(1)
        rotated("q", rq_t, "rq")
        fox_scores(2)
        unit(UNIT["rv"], XT, "x")
        fox_values(2)
        rotated("k", rk_t, "rk")
        fox_scores(3)
        unit(UNIT["fog"], XT, "w")
        fox_values(3)
        pe.wait_ge(*roped.at("k"))
        pe.wait_ge(*set_done(UNIT["rv"]))

        def ret_scores(a):
            claim(a % 2, ("rs", a))
            pe.matmul(bank[:, a % 2, 0:S], rk_t[:, a, 0:P], rq_t[:, a, :], start=True, stop=True,
                      skip_group_check=True)
            pe.matmul(bank[:, a % 2, S:S + P], rk_t[:, a, P:S], rq_t[:, a, P:S], start=True, stop=True,
                      skip_group_check=True).then_inc(filled[a % 2], 1)

        ret_scores(0)
        ret_scores(1)

        def ret_values(a):
            n = 2 + a // 2
            pe.wait_ge(*decayed.at(a))
            if a % 2 == 0:
                claim(n, ("o", ("r", a // 2)))
            st = hn[:, a // 2, (a % 2) * NB:(a % 2) * NB + S + P]
            pe.matmul(bank[:, n, (a % 2) * S:(a % 2 + 1) * S], rv_nat[:, 0, a * P:(a + 1) * P], st[:, 0:S],
                      start=True, stop=False, skip_group_check=True)
            mm = pe.matmul(bank[:, n, (a % 2) * S + P:(a % 2 + 1) * S], rv_nat[:, 1, a * P:(a + 1) * P],
                           st[:, S:S + P], start=False, stop=True, skip_group_check=True)
            if a % 2 == 1:
                mm.then_inc(filled[n], 1)

        def amid_rg():
            head_sums("fo", col_halves, fk_t)
            ret_values(0)
            ret_values(1)
            head_back("fo", flat(fk_t))
            ret_scores(2)
            ret_scores(3)

        unit(UNIT["rg"], XT, "w", mid=amid_rg)
        ret_values(2)
        ret_values(3)
        head_sums("ro", ones[:, 0:1], rk_t)
        head_back("ro")
        unit(UNIT["out2"], YT_, "x", (yt_ready.at("fo"), yt_ready.at("ro")), mid=lambda: row("gate_m", 2, 2))
        pe.wait_ge(*mod_ready.at(1))
        unit(UNIT["out2"] + 1, YT_, "x", mid=lambda: row("scale_f", 4, 2))
        row("shift_f", 3, 2)
        row("gate_f", 5, 0)
        transposes("mlp2")
        mlp(2, "mlp2")

    @block.scalar
    def _(act):
        steps = [0]

        def step(ins):
            steps[0] += 1
            ins.then_inc(act_step, 1)
            act.wait_ge(act_step, steps[0])

        def hi_half(k, i=None, last=False):
            if k + (24 if last else 0) >= NH:
                return
            s = k % RING
            i = 3 if last else (0 if i is None else i)
            act.wait_ge(landed[s], 16 * (k // RING + 1) + 32 * i)
            if k >= RING:
                act.wait_ge(half_used, k - RING + 1 + 8 * i)
            act.activation(hi[:, s], raw[:, s], ACT.Copy).then_inc(hi_ready, 1)

        def copy0(u, dst, mid=None):
            hi_half(2 * u + 4)
            if mid is not None:
                mid()
            act.wait_ge(bank0_done, u + 1)
            src = gemm[:, 2 * (u % 2), :]
            act.activation(dst, cut(src, 2) if len(dst.shape) == 3 else src, ACT.Copy)\
                .then_inc(evacuated[u % 2], 1)
            hi_half(2 * u + 5)

        def stream(u):
            hi_half(2 * u + 4)
            hi_half(2 * u + 5)

        def sum_squares(n, t, src):
            c = squares.order.index((n, t))
            act.activation(hn[:, t, :], src, ACT.Square, accum_out=stat[:, c:c + 1])\
                .then_inc(*squares.up((n, t)))

        def residual_squares(n, u, tail=True):
            for t in range(T):
                act.wait_ge(*set_done(u, t + 1))
                sum_squares(n, t, h[:, t, :])
            if tail:
                hi_half(2 * u + 5)

        def turned_hi_parts(n, dst):
            for t in range(T):
                for j in range(2):
                    act.wait_ge(*fill((n, t, j)))
                    act.activation(dst[:, j * HC:(j + 1) * HC, t * P:(t + 1) * P], cut(bank[:, turn_bank(t, j), :], HC),
                                   ACT.Copy).then_inc(*turned_hi.up((n, t, j)))

        def keep_turned(grp, dst, part=0):
            act.wait_ge(*fill(("t", grp, part)))
            n = dst.shape[1]
            act.activation(dst, cut(bank[:, 2, :], 4)[:, 0:n, :], ACT.Copy).then_inc(freed[2], 1)

        def keep_row(name, dst, first, bias=0.0):
            for j in range(2):
                act.wait_ge(*fill(("row", name, j)))
                act.activation(dst[:, j * NB:(j + 1) * NB], bank[:, first + j, :], ACT.Copy, bias=bias)\
                    .then_inc(freed[first + j], 1)

        def head_roots(name, n, width):
            act.wait_ge(*fill(("h", name)))
            act.activation(head_inv[:, 0:n], bank[:, 0, 0:n], ACT.Sqrt, bias=eps[:, :], scale=1.0 / width)\
                .then_inc(freed[0], 1)

        def split_hi(label, dst, src, *wait):
            act.wait_ge(*wait)
            act.activation(dst, src, ACT.Copy).then_inc(*yt_hi_ready.up(label))

        act.dma_start(flip_m, d["flip"]).then_inc(loaded["rel"], 16)
        act.dma_start(bucket_m[0:BUCKETS, :], d["bucket"]).then_inc(loaded["rel"], 16)
        act.dma_start(rel[0:BUCKETS, :], d["rel_bias"]).then_inc(loaded["rel"], 16)
        act.dma_start(gain, d["gains"][0:1, :].to_broadcast((P, D))).then_inc(loaded["gain_mix0"], 16)
        act.dma_start(ident[:, :], d["ident"]).then_inc(loaded["ident"], 16)
        act.wait_ge(loaded["x"], 32)
        for t in range(T):
            sum_squares("mix0", t, h[:, t, :])
        act.wait_ge(*fill("bias_row"))
        act.activation(bias_row[0:4, :], bank[0:4, 0, 0:384], ACT.Copy).then_inc(freed[0], 1)
        hi_half(0)
        turned_hi_parts("mix0", xt_hi)
        for k in range(1, RING):
            hi_half(k)
        act.wait_ge(*lam_sums.at(1))
        for n in range(2):
            act.activation(lam[:, 2 + n:3 + n], lam[:, n:n + 1], ACT.Exp).then_inc(*lam_exp.up(n))
        act.wait_ge(loaded["mem"], 32)
        for t in range(T):
            act.wait_ge(*fill(("mix0", t, 1)))
            sum_squares("mem", t, mem_rows[:, t, :])
        copy0(UNIT["l0_u"], u_nat[:, 0, :])
        copy0(UNIT["l0_q"], q_t[:, 0:2, :])
        for b in range(2):
            act.wait_ge(*fill(("pool_t", b)))
            act.activation(pool_t[:, 2 * b:2 * b + 2, :], cut(bank[:, b, :], 2), ACT.Copy)\
                .then_inc(freed[b], 1)
        copy0(UNIT["l0_k"], k_t[:, 0:2, :], mid=lambda: turned_hi_parts("mem", mt_hi))
        for b in range(2):
            act.wait_ge(*fill(("pool_y", b)))
            for a in range(2):
                g = 2 * b + a
                ins = act.activation(pool_y[:, g, :], cut(bank[:, 2 + b, :], 2)[:, a, :], ACT.Copy,
                                     scale=col("pool_scale", g))
            ins.then_inc(freed[2 + b], 1)
            split_hi(("pool", b), yt_hi[:, 2 * b:2 * b + 2, :], pool_y[:, 2 * b:2 * b + 2, :],
                     *read(("pool_y", b)))
        act.wait_ge(*yt_ready.at(("pool", 1)))
        copy0(UNIT["l0_v"], v_nat[:, 0, :])
        for g in range(4):
            hg, qt = g // 2, g % 2
            nk = P * (qt + 1)
            e = hn[:, g % 2, :].rearrange("p (s a k) -> p s a k", s=2, a=2)
            act.wait_ge(*shift_ready.at(("d", g)))
            for s in range(2):
                for a in range(2):
                    n = 4 * g + 2 * s + a
                    ins = act.activation(e[:, s, a, 0:nk], e[:, s, a, 0:nk], ACT.Exp, bias=shift[:, n:n + 1],
                                         accum_out=total[:, n:n + 1])
            ins.then_inc(*diff_exp.up(g))
            u = UNIT["kv0"] + g
            copy0(u, kv_k[:, 4 * g:4 * g + 2, :] if g < 2 else kv_v[:, 0, (g - 2) * NB:(g - 1) * NB])
            keep_turned(("d", g), a_t[:, g % 2, 0:2 * (qt + 1), :])
            if qt == 1:
                act.wait_ge(*fill(("o", ("d", hg))))
                act.activation(diff_o[:, 2 * hg:2 * hg + 2, :], cut(bank[:, 3, :], 2), ACT.Copy)\
                    .then_inc(freed[3], 1)
        act.wait_ge(*read(("o", ("d", 0))))
        act.wait_ge(*read(("o", ("d", 1))))
        act.activation(diff_sq, diff_o, ACT.Square).then_inc(*hsq.up("d"))
        head_roots("d", 8, P)
        for b in range(2):
            split_hi(("diff", b), yt_hi[:, 4 + 2 * b:6 + 2 * b, :], diff_o[:, 2 * b:2 * b + 2, :],
                     *hnormed.at("d"))
        act.wait_ge(loaded["c"], 16)
        act.activation(c_tmp, c_act, ACT.Exp, scale=-1.0).then_inc(*c_exp.up(0))
        stream(UNIT["l0_out"])
        hi_half(2 * UNIT["l0_out"] + 6)

        def cross(x, filler=None):
            u = UNIT["q" + x[1]]
            def exps(g):
                act.wait_ge(*shift_ready.at((x, g)))
                e = cut(hn[:, g // 2, (g % 2) * NB:(g % 2 + 1) * NB], 2)
                for a in range(2):
                    n = 4 * g + a
                    ins = act.activation(e[:, a, :], cut(bank[:, g % 2, :], 2)[:, a, :], ACT.Exp,
                                         bias=shift[:, n:n + 1], scale=1.0 / 16, accum_out=total[:, n:n + 1])
                ins.then_inc(freed[g % 2], 1)

            def first_exps():
                exps(0)
                exps(1)

            copy0(u, cq_t[:, 0:2, :])
            copy0(u + 1, cq_t[:, 4:6, :], mid=first_exps)
            if filler is not None:
                copy0(UNIT[filler], kv_v[:, 0, NB:D])
            for g in range(4):
                hg, qt = g // 2, g % 2
                keep_turned((x, g), p_t[:, g % 2])
                if g + 2 < 4:
                    exps(g + 2)
                split_hi((x, g), yt_hi[:, 4 * hg:4 * hg + 4, qt * P:(qt + 1) * P], cut(bank[:, 3, :], 4),
                         *fill(("o", (x, g))))
            u = UNIT["o" + x[1]]
            hi_half(2 * u + 4)
            if x == "x1":
                keep_row("shift_m", shift_row, 0)
            hi_half(2 * u + 5)
            hi_half(2 * u + 6)
            if x == "x1":
                keep_row("scale_m", scale_row, 2, bias=1.0)

        def mlp_chunk(m, i, last=False):
            for j in range(4):
                u = UNIT[f"mlp{m}"] + j
                hi_half(2 * u + 4, i, last)
                if j < 2:
                    s = u % 2
                    r = hn[:, j, :]
                    act.wait_ge(bank0_done, u + 1 + 4 * i)
                    act.activation(r[:, 0:NB], gemm[:, 2 * s, :], ACT.Relu).then_inc(evacuated[s], 1)
                    act.wait_ge(half_used, 2 * u + 2 + 8 * i)
                    act.activation(r[:, NB:D], gemm[:, 2 * s + 1, :], ACT.Relu).then_inc(evacuated[s], 1)
                    act.wait_ge(evacuated[s], 2 * (u // 2) + 2 + 4 * i)
                    act.activation(yt_hi[:, 4 * j:4 * j + 4, :], cut(r, 4), ACT.Square)\
                        .then_inc(hid_hi[m], 1)
                hi_half(2 * u + 5, i, last)

        def mlp(m):
            if m < 2:
                with act.Fori(0, 4) as i:
                    mlp_chunk(m, i)
            else:
                with act.Fori(0, 3) as i:
                    mlp_chunk(m, i)
                mlp_chunk(m, 3, last=True)

        residual_squares("x0", UNIT["l0_out"] + 1)
        turned_hi_parts("x0", xt_hi)
        cross("x0")
        residual_squares("mlp0", UNIT["o0"] + 1)
        copy0(UNIT["kv1b"], kv_k[:, 4:6, :], mid=lambda: turned_hi_parts("mlp0", xt_hi))
        mlp(0)
        residual_squares("mix1", UNIT["mlp0"] + 15, tail=False)
        copy0(UNIT["kv1a"], kv_k[:, 0:2, :], mid=lambda: turned_hi_parts("mix1", xt_hi))
        for b in range(2):
            u = UNIT["conv"] + 3 * b
            if b == 1:
                act.wait_ge(*conv_z.at(0))
            copy0(u, gate_c[:, 0:2, :])
            stream(u + 1)
            stream(u + 2)
            split_hi(("conv", b), yt_hi[:, 4 * b:4 * b + 4, :], conv_y, *conv_y_ready.at(b))
        stream(UNIT["conv_out"])
        hi_half(2 * UNIT["conv_out"] + 6)
        residual_squares("x1", UNIT["conv_out"] + 1)
        copy0(UNIT["kv1c"], kv_v[:, 0, 0:NB], mid=lambda: turned_hi_parts("x1", xt_hi))
        cross("x1", "kv1d")
        residual_squares("mlp1", UNIT["o1"] + 1)
        turned_hi_parts("mlp1", xt_hi)
        mlp(1)

        residual_squares("final", UNIT["mlp1"] + 15, tail=False)
        for t in range(T):
            act.wait_ge(*final_done.at(t))
            sum_squares("mix2", t, h[:, t, :])
        act.wait_ge(loaded["ff"], 16)
        act.activation(ff_hi[:, :, :], ff_raw[:, :, :], ACT.Copy).then_inc(*ff_hi_ready.up(0))
        turned_hi_parts("mix2", xt_hi)

        def head_squares(name, dst, src, *waits):
            for wait in waits:
                act.wait_ge(*wait)
            act.activation(dst, src, ACT.Square).then_inc(*hsq.up(name))

        copy0(UNIT["fq"], fq_t[:, 0:2, :])
        head_squares("fq", hn[:, 0, :], flat(fq_t), set_done(UNIT["fq"]))
        copy0(UNIT["fk"], fk_t[:, 0:2, :], mid=lambda: head_roots("fq", 16, 64))
        head_squares("fk", hn[:, 1, :], flat(fk_t), set_done(UNIT["fk"]))
        act.wait_ge(*logf_abs.at(0))
        step(act.activation(logf[:, 2, :], logf[:, 1, :], ACT.Exp, scale=-1.0))
        act.activation(logf[:, 3, :], logf[:, 2, :], ACT.Ln, bias=ones[:, 0:1]).then_inc(*logf_ln.up(0))
        copy0(UNIT["fv"], fv_nat[:, 0, :], mid=lambda: head_roots("fk", 16, 64))

        def fox_exps(g):
            qt = g % 2
            nk = P * (qt + 1)
            e = cut(hn[:, g % 2, :], 4)
            act.wait_ge(*shift_ready.at(("f", g)))
            for a in range(4):
                n = 4 * g + a
                ins = act.activation(e[:, a, 0:nk], cut(bank[:, a // 2, :], 2)[:, a % 2, 0:nk], ACT.Exp,
                                     bias=shift[:, n:n + 1], accum_out=total[:, n:n + 1])
                if a % 2 == 1:
                    ins.then_inc(freed[a // 2], 1)

        def fox_kept(g):
            hg, qt = g // 2, g % 2
            for part in range(qt + 1):
                keep_turned(("f", g), e_t[:, 4 * part:4 * part + 4, :], part)
            if qt == 1:
                act.wait_ge(*fill(("o", ("f", hg))))
                act.activation(fq_t[:, 2 * hg:2 * hg + 2, :], cut(bank[:, 3, :], 2), ACT.Copy)\
                    .then_inc(freed[3], 1)

        fox_exps(0)
        copy0(UNIT["rq"], rq_t[:, 0:2, :])
        fox_kept(0)
        fox_exps(1)
        copy0(UNIT["rk"], rk_t[:, 0:2, :])
        fox_kept(1)
        fox_exps(2)
        copy0(UNIT["rv"], rv_nat[:, 0, :])
        fox_kept(2)
        fox_exps(3)
        u = UNIT["fog"]
        hi_half(2 * u + 4)
        for b in range(2):
            act.wait_ge(*((bank0_done, u + 1) if b == 0 else (half_used, 2 * u + 2)))
            act.activation(fog_t[:, 2 * b:2 * b + 2, :], cut(gemm[:, 2 * (u % 2) + b, :], 2), ACT.Exp, scale=-1.0)\
                .then_inc(evacuated[u % 2], 1)
        hi_half(2 * u + 5)
        fox_kept(3)
        head_squares("fo", flat(fk_t), flat(fq_t), read(("o", ("f", 0))), read(("o", ("f", 1))))

        def keep_ret(b):
            act.wait_ge(*fill(("o", ("r", b))))
            act.activation(rq_t[:, 2 * b:2 * b + 2, :], cut(bank[:, 2 + b, :], 2), ACT.Copy)\
                .then_inc(freed[2 + b], 1)

        u = UNIT["rg"]
        head_roots("fo", 16, 64)
        hi_half(2 * u + 4)
        keep_ret(0)
        split_hi("fo", yt_hi[:, 0:4, :], fq_t, *hnormed.at("fo"))
        hi_half(2 * u + 5)
        keep_ret(1)
        head_squares("ro", flat(rk_t), flat(rq_t), read(("o", ("r", 0))), read(("o", ("r", 1))))
        act.wait_ge(*rg_kept.at(0))
        act.activation(rg_exp_t, rg_t, ACT.Exp, scale=-1.0).then_inc(*rg_exp.up(0))
        head_roots("ro", 8, P)
        split_hi("ro", yt_hi[:, 4:8, :], rq_t, *hnormed.at("ro"))
        keep_row("gate_m", gate_m_row, 2)
        stream(UNIT["out2"])
        hi_half(2 * UNIT["out2"] + 6)
        keep_row("scale_f", gain, 2, bias=1.0)
        residual_squares("mlp2", UNIT["out2"] + 1)
        keep_row("shift_f", shift_row, 2)
        keep_row("gate_f", gate_f_row, 0)
        turned_hi_parts("mlp2", xt_hi)
        mlp(2)

    @block.vector
    def _(dve):
        steps = [0]
        gate_steps = [0]

        def step(ins, wait=True):
            steps[0] += 1
            ins.then_inc(vec_step, 1)
            if wait:
                dve.wait_ge(vec_step, steps[0])

        def lo_half(k, i=None, last=False):
            if k + (24 if last else 0) >= NH:
                return
            s = k % RING
            i = 3 if last else (0 if i is None else i)
            dve.wait_ge(hi_ready, k + 1 + 8 * i)
            dve.tensor_tensor(lo[:, s], raw[:, s], hi[:, s].bitcast(F32), ALU.subtract).then_inc(lo_ready, 1)

        def copy1(u, dst, mid=None):
            lo_half(2 * u + 4)
            if mid is not None:
                mid()
            dve.wait_ge(half_used, 2 * u + 2)
            src = gemm[:, 2 * (u % 2) + 1, :]
            dve.tensor_copy(dst, cut(src, 2) if len(dst.shape) == 3 else src).then_inc(evacuated[u % 2], 1)
            lo_half(2 * u + 5)

        def add_residual(u, n, gate=None, i=None, last=False, tail=True):
            k = 0 if i is None else i
            lo_half(2 * u + 4, i, last)
            blk = slice(n * NB, (n + 1) * NB)
            for t in range(T):
                dve.wait_ge(*((bank0_done, u + 1 + 4 * k) if t == 0 else (half_used, 2 * u + 2 + 8 * k)))
                src = gemm[:, 2 * (u % 2) + t, :]
                if gate is not None:
                    dve.tensor_tensor(gated[:, t, :], src, gate[:, blk], ALU.mult).then_inc(gated_done, 1)
                    gate_steps[0] += 1
                    dve.wait_ge(gated_done, gate_steps[0] + 4 * k)
                    src = gated[:, t, :]
                dve.tensor_tensor(h[:, t, blk], h[:, t, blk], src, ALU.add).then_inc(evacuated[u % 2], 1)
            if tail:
                lo_half(2 * u + 5, i, last)

        def scaled_rows(n, src):
            for t in range(T):
                c = rstd_done.order.index((n, t))
                dve.wait_ge(*rstd_done.at((n, t)))
                if n == "mix0" or n == "mem" or n in GAINS:
                    dve.wait_ge(loaded["gain_" + n], 16)
                ins = dve.scalar_tensor_tensor(hn[:, t, :], src[:, t, :], rstd[:, c:c + 1],
                                               scale_row if n == "mix2" else gain, ALU.mult, ALU.mult)
                if n in ("mix2", "mlp2"):
                    step(ins)
                    ins = dve.tensor_tensor(hn[:, t, :], hn[:, t, :], shift_row, ALU.add)
                ins.then_inc(*normed.up((n, t)))

        def turned_lo_parts(n, dst, upper):
            for t in range(T):
                for j in range(2):
                    dve.wait_ge(*turned_hi.at((n, t, j)))
                    part = (slice(None), slice(j * HC, (j + 1) * HC), slice(t * P, (t + 1) * P))
                    b = turn_bank(t, j)
                    dve.tensor_tensor(dst[part], cut(bank[:, b, :], HC), upper[part].bitcast(F32),
                                      ALU.subtract).then_inc(freed[b], 1)

        def split_lo(label, part, src):
            dve.wait_ge(*yt_hi_ready.at(label))
            dve.tensor_tensor(yt_lo[part], src, yt_hi[part].bitcast(F32), ALU.subtract)\
                .then_inc(*yt_ready.up(label))

        def head_inverse(name, n, wide=None):
            dve.wait_ge(*read(("h", name)))
            ins = dve.reciprocal(head_inv[:, 0:n], head_inv[:, 0:n])
            if wide is not None:
                step(ins)
                src = head_inv[:, 0:n].rearrange("p (a b) -> p a b", b=1).to_broadcast((P, n, 64))
                ins = dve.tensor_copy(cut(wide, n), src)
            ins.then_inc(*hinverse.up(name))

        def head_norm(name, x, gains, gate=None):
            for b in range(2):
                dve.wait_ge(*fill(("b", name, b)))
                for c in (2 * b, 2 * b + 1):
                    ins = dve.scalar_tensor_tensor(x[:, c, :], x[:, c, :], gains[c % len(gains)],
                                                   cut(bank[:, b, :], 2)[:, c % 2, :], ALU.mult, ALU.mult)
                    if c % 2 == 0:
                        step(ins, wait=False)
                ins.then_inc(freed[b], 1)
            dve.wait_ge(*read(("b", name, 0)))
            dve.wait_ge(*read(("b", name, 1)))
            if gate is None:
                dve.engine_nop().then_inc(*hnormed.up(name))
            else:
                dve.tensor_tensor(x, x, gate, ALU.mult).then_inc(*hnormed.up(name))

        def recip_total(g, n):
            cs = slice(4 * g, 4 * g + n)
            step(dve.reciprocal(inv[:, cs], total[:, cs]))

        scaled_rows("mix0", h)
        lo_half(0)
        turned_lo_parts("mix0", xt_lo, xt_hi)
        for k in range(1, RING):
            lo_half(k)
        dve.wait_ge(loaded["consts"], 32)
        dve.wait_ge(loaded["lam"], 16)
        for n in range(2):
            dve.tensor_tensor_reduce(lam_in[:, 2 * n, :], lam_in[:, 2 * n, :], lam_in[:, 2 * n + 1, :], 1.0, 0.0,
                                     ALU.mult, ALU.add, lam[:, n:n + 1]).then_inc(*lam_sums.up(n))
        step(dve.tensor_scalar(col("subln"), col("subln"), 1.0 - LAMBDA_INIT, None, ALU.mult), wait=False)
        step(dve.tensor_scalar(col("qg"), col("qg"), 64.0 ** -0.5, None, ALU.mult), wait=False)
        for t in range(T):
            dve.wait_ge(*fill(("mix0", t, 1)))
        scaled_rows("mem", mem_rows)
        dve.wait_ge(*lam_exp.at(1))
        dve.scalar_tensor_tensor(lam[:, 4:5], lam[:, 3:4], -LAMBDA_INIT, lam[:, 2:3], ALU.add, ALU.subtract)\
            .then_inc(*lam_ready.up(0))
        copy1(UNIT["l0_u"], u_nat[:, 1, :])
        for n, dst in ((0, bias1[:, 0:2, :]), (1, bias1[:, 2:4, :]), (2, bias0)):
            dve.wait_ge(*fill(("bias", n)))
            dve.tensor_copy(dst, cut(bank[:, n, :], dst.shape[1])).then_inc(freed[n], 1)
        copy1(UNIT["l0_q"], q_t[:, 2:4, :])
        copy1(UNIT["l0_k"], k_t[:, 2:4, :], mid=lambda: turned_lo_parts("mem", mt_lo, mt_hi))
        for b in range(2):
            part = (slice(None), slice(2 * b, 2 * b + 2), slice(None))
            split_lo(("pool", b), part, pool_y[part])
        dve.wait_ge(*yt_ready.at(("pool", 1)))
        copy1(UNIT["l0_v"], v_nat[:, 1, :])
        dve.wait_ge(*bias_masked.at(1))
        dve.wait_ge(*lam_ready.at(0))
        for g in range(4):
            hg, qt = g // 2, g % 2
            nk = P * (qt + 1)
            e = hn[:, g % 2, :].rearrange("p (s a k) -> p s a k", s=2, a=2)
            bias = bias1 if qt else bias0
            for s in range(2):
                dve.wait_ge(*fill(("s", ("d", g), s)))
                dve.scalar_tensor_tensor(e[:, s, :, 0:nk], cut(bank[:, s, :], 2)[:, :, 0:nk], 64.0 ** -0.5,
                                         bias[:, 2 * hg:2 * hg + 2, 0:nk], ALU.mult, ALU.add)\
                    .then_inc(freed[s], 1)
            cs = slice(4 * g, 4 * g + 4)
            dve.wait_ge(*read(("s", ("d", g), 1)))
            step(dve.tensor_reduce(peak[:, cs], cut(hn[:, g % 2, :], 4)[:, :, 0:nk], AX_X, ALU.max))
            dve.tensor_scalar(shift[:, cs], peak[:, cs], -1.0, None, ALU.mult)\
                .then_inc(*shift_ready.up(("d", g)))
            u = UNIT["kv0"] + g
            lo_half(2 * u + 4)
            dve.wait_ge(*diff_exp.at(g))
            recip_total(g, 4)
            step(dve.tensor_scalar(inv[:, 4 * g + 2:4 * g + 4], inv[:, 4 * g + 2:4 * g + 4], lam[:, 4:5], None,
                                   ALU.mult), wait=False)
            for a in range(2):
                step(dve.tensor_scalar(e[:, 0, a, 0:nk], e[:, 0, a, 0:nk], inv[:, 4 * g + a:4 * g + a + 1], None,
                                       ALU.mult), wait=(a == 1))
            for a in range(2):
                ins = dve.scalar_tensor_tensor(e[:, 0, a, 0:nk], e[:, 1, a, 0:nk],
                                               inv[:, 4 * g + 2 + a:4 * g + 3 + a], e[:, 0, a, 0:nk],
                                               ALU.mult, ALU.add)
            ins.then_inc(*probs_ready.up(("d", g)))
            dve.wait_ge(half_used, 2 * u + 2)
            if g < 2:
                dve.tensor_copy(kv_k[:, 4 * g + 2:4 * g + 4, :], cut(gemm[:, 2 * (u % 2) + 1, :], 2))\
                    .then_inc(evacuated[u % 2], 1)
            else:
                dve.tensor_copy(kv_v[:, 1, (g - 2) * NB:(g - 1) * NB], gemm[:, 2 * (u % 2) + 1, :])\
                    .then_inc(evacuated[u % 2], 1)
            lo_half(2 * u + 5)
        head_inverse("d", 8)
        head_norm("d", diff_o, [col("subln")])
        for b in range(2):
            split_lo(("diff", b), (slice(None), slice(4 + 2 * b, 6 + 2 * b), slice(None)),
                     diff_o[:, 2 * b:2 * b + 2, :])
        dve.wait_ge(*c_exp.at(0))
        step(dve.tensor_scalar(c_tmp, c_tmp, 1.0, None, ALU.add))
        step(dve.reciprocal(c_tmp, c_tmp))
        dve.tensor_tensor(c_act, c_act, c_tmp, ALU.mult).then_inc(ada_kept, 1)
        add_residual(UNIT["l0_out"], 0)
        add_residual(UNIT["l0_out"] + 1, 1, tail=False)

        def cross(x, filler=None):
            u = UNIT["q" + x[1]]
            def shifts(g):
                cs = slice(4 * g, 4 * g + 2)
                dve.wait_ge(*fill(("s", (x, g), 0)))
                step(dve.tensor_reduce(peak[:, cs], cut(bank[:, g % 2, :], 2), AX_X, ALU.max))
                dve.tensor_scalar(shift[:, cs], peak[:, cs], -1.0 / 16, None, ALU.mult)\
                    .then_inc(*shift_ready.up((x, g)))

            def probs(g):
                e = cut(hn[:, g // 2, (g % 2) * NB:(g % 2 + 1) * NB], 2)
                dve.wait_ge(*read(("s", (x, g), 0)))
                recip_total(g, 2)
                for a in range(2):
                    ins = dve.tensor_scalar(e[:, a, :], e[:, a, :], inv[:, 4 * g + a:4 * g + a + 1], None,
                                            ALU.mult)
                    if a == 0:
                        step(ins, wait=False)
                ins.then_inc(*probs_ready.up((x, g)))

            def first_probs():
                shifts(0)
                shifts(1)
                probs(0)
                probs(1)

            copy1(u, cq_t[:, 2:4, :])
            copy1(u + 1, cq_t[:, 6:8, :], mid=first_probs)
            if filler is not None:
                copy1(UNIT[filler], kv_v[:, 1, NB:D])
            for g in range(4):
                hg, qt = g // 2, g % 2
                if g + 2 < 4:
                    shifts(g + 2)
                    probs(g + 2)
                part = (slice(None), slice(4 * hg, 4 * hg + 4), slice(qt * P, (qt + 1) * P))
                dve.wait_ge(*yt_hi_ready.at((x, g)))
                dve.tensor_tensor(yt_lo[part], cut(bank[:, 3, :], 4), yt_hi[part].bitcast(F32), ALU.subtract)\
                    .then_inc(freed[3], 1)
            add_residual(UNIT["o" + x[1]], 0)
            add_residual(UNIT["o" + x[1]] + 1, 1, tail=False)

        def ada_columns(m, i, a):
            dve.wait_ge(ada_landed, 16 * (8 * m + a + 1) + 32 * i)
            for n in range(ADA_COLS):
                ins = dve.tensor_tensor_reduce(ada[:, n, :], ada[:, n, :], c_act, 1.0, 0.0, ALU.mult, ALU.add,
                                               mod_part[:, ADA_COLS * a + n:ADA_COLS * a + n + 1])
            ins.then_inc(ada_used, 1)

        def mlp_chunk(m, i, last=False):
            for j in range(4):
                u = UNIT[f"mlp{m}"] + j
                if j < 2:
                    lo_half(2 * u + 4, i, last)
                    if m < 2:
                        if j == 0:
                            dve.wait_ge(ada_kept, 4 * m + 1 + i)
                        ada_columns(m, i, j)
                    r = hn[:, j, :]
                    dve.wait_ge(hid_hi[m], 2 * i + j + 1)
                    dve.tensor_tensor(r, r, r, ALU.mult).then_inc(hid_sq[m], 1)
                    dve.wait_ge(hid_sq[m], 2 * i + j + 1)
                    part = yt_lo[:, 4 * j:4 * j + 4, :]
                    dve.tensor_tensor(part, cut(r, 4), yt_hi[:, 4 * j:4 * j + 4, :].bitcast(F32), ALU.subtract)\
                        .then_inc(hid_ready[m], 1)
                    lo_half(2 * u + 5, i, last)
                else:
                    add_residual(u, j - 2, gate_f_row if m == 2 else None, i, last)
            if m < 2:
                dve.wait_ge(ada_used, 8 * m + 2 * i + 2)
                dve.tensor_copy(mod[:, bass.ds(6 * i + 24 * m, 6)], mod_part[:, :]).then_inc(ada_kept, 1)

        def mlp(m):
            if m < 2:
                with dve.Fori(0, 4) as i:
                    mlp_chunk(m, i)
            else:
                before = gate_steps[0]
                with dve.Fori(0, 3) as i:
                    mlp_chunk(m, i)
                gate_steps[0] = before
                mlp_chunk(m, 3, last=True)

        def norm(n, u):
            scaled_rows(n, h)
            turned_lo_parts(n, xt_lo, xt_hi)
            lo_half(2 * u + 5)

        b_ada = cols[:, COL["b_ada"]]
        norm("x0", UNIT["l0_out"] + 1)
        cross("x0")
        scaled_rows("mlp0", h)
        lo_half(2 * UNIT["o0"] + 7)
        copy1(UNIT["kv1b"], kv_k[:, 6:8, :], mid=lambda: turned_lo_parts("mlp0", xt_lo, xt_hi))
        mlp(0)
        scaled_rows("mix1", h)
        copy1(UNIT["kv1a"], kv_k[:, 2:4, :], mid=lambda: turned_lo_parts("mix1", xt_lo, xt_hi))
        dve.wait_ge(ada_kept, 5)
        dve.tensor_tensor(mod[:, 0:24], mod[:, 0:24], b_ada[:, 0:24], ALU.add).then_inc(*mod_ready.up(0))
        step(dve.memset(z_pad[:, :, 0:2], 0.0))
        for b in range(2):
            u = UNIT["conv"] + 3 * b
            copy1(u, gate_c[:, 2:4, :])
            dve.wait_ge(*set_done(u))
            lo_half(2 * u + 6)
            for n in range(2):
                dve.wait_ge(*((bank0_done, u + 2) if n == 0 else (half_used, 2 * u + 4)))
                dve.tensor_tensor(z_pad[:, 2 * n:2 * n + 2, 2:], gate_c[:, 2 * n:2 * n + 2, :],
                                  cut(gemm[:, 2 * ((u + 1) % 2) + n, :], 2), ALU.mult)\
                    .then_inc(evacuated[(u + 1) % 2], 1)
            dve.wait_ge(*set_done(u + 1))
            dve.engine_nop().then_inc(*conv_z.up(b))
            lo_half(2 * u + 7)
            for tap in range(3):
                for c in range(4):
                    wcol = col("conv", 8 * tap + 4 * b + c)
                    z = z_pad[:, c, tap:tap + S]
                    if tap == 0:
                        ins = dve.tensor_scalar(conv_y[:, c, :], z, wcol, None, ALU.mult)
                    else:
                        ins = dve.scalar_tensor_tensor(conv_y[:, c, :], z, wcol, conv_y[:, c, :], ALU.mult,
                                                       ALU.add)
                    step(ins, wait=(c == 3))
            lo_half(2 * u + 8)
            for n in range(2):
                dve.wait_ge(*((bank0_done, u + 3) if n == 0 else (half_used, 2 * u + 6)))
                y = conv_y[:, 2 * n:2 * n + 2, :]
                dve.tensor_tensor(y, y, cut(gemm[:, 2 * (u % 2) + n, :], 2), ALU.mult)\
                    .then_inc(evacuated[u % 2], 1)
            dve.wait_ge(*set_done(u + 2))
            dve.engine_nop().then_inc(*conv_y_ready.up(b))
            split_lo(("conv", b), (slice(None), slice(4 * b, 4 * b + 4), slice(None)), conv_y)
            lo_half(2 * u + 9)
        add_residual(UNIT["conv_out"], 0)
        add_residual(UNIT["conv_out"] + 1, 1, tail=False)
        scaled_rows("x1", h)
        lo_half(2 * UNIT["conv_out"] + 7)
        copy1(UNIT["kv1c"], kv_v[:, 1, 0:NB], mid=lambda: turned_lo_parts("x1", xt_lo, xt_hi))
        cross("x1", "kv1d")
        norm("mlp1", UNIT["o1"] + 1)
        mlp(1)

        for t in range(T):
            c = rstd_done.order.index(("final", t))
            dve.wait_ge(*rstd_done.at(("final", t)))
            dve.wait_ge(loaded["gain_final"], 16)
            dve.scalar_tensor_tensor(h[:, t, :], h[:, t, :], rstd[:, c:c + 1], gain, ALU.mult, ALU.mult)\
                .then_inc(*final_done.up(t))
        dve.wait_ge(*read(("row", "scale_m", 1)))
        dve.wait_ge(*read(("row", "shift_m", 1)))
        scaled_rows("mix2", h)
        dve.wait_ge(ada_kept, 9)
        dve.tensor_tensor(mod[:, 24:48], mod[:, 24:48], b_ada[:, 24:48], ALU.add).then_inc(*mod_ready.up(1))
        dve.wait_ge(*ff_hi_ready.at(0))
        dve.tensor_tensor(ff_lo[:, :, :], ff_raw[:, :, :], ff_hi[:, :, :].bitcast(F32), ALU.subtract)\
            .then_inc(*ff_ready.up(0))
        turned_lo_parts("mix2", xt_lo, xt_hi)
        copy1(UNIT["fq"], fq_t[:, 2:4, :])
        copy1(UNIT["fk"], fk_t[:, 2:4, :], mid=lambda: head_inverse("fq", 16, hn[:, 0, :]))
        head_norm("fq", fq_t, [col("qg")])
        dve.wait_ge(*fill("ff"))
        b_forget = cols[:, COL["b_forget"]]
        step(dve.tensor_tensor(logf[:, 0, 0:8], bank[:, 2, 0:8], b_forget, ALU.add), wait=False)
        dve.tensor_tensor(logf[:, 0, 8:16], bank[:, 2, 8:16], b_forget, ALU.add).then_inc(freed[2], 1)
        dve.wait_ge(*read("ff"))
        dve.scalar_tensor_tensor(logf[:, 1, :], logf[:, 0, :], -1.0, logf[:, 0, :], ALU.mult, ALU.max)\
            .then_inc(*logf_abs.up(0))
        dve.wait_ge(*logf_ln.at(0))
        dve.scalar_tensor_tensor(logf[:, 4, :], logf[:, 0, :], 0.0, logf[:, 3, :], ALU.min, ALU.subtract)\
            .then_inc(*logf_ready.up(0))

        def fox_gates():
            head_inverse("fk", 16, hn[:, 1, :])
            dve.wait_ge(*fill("cum"))
            step(dve.tensor_copy(logf[:, 5, :], bank[:, 2, 0:16]), wait=False)
            dve.tensor_scalar(cum_rows[:, :], bank[0:8, 2, P:P + S], -1.0, None, ALU.mult).then_inc(freed[2], 1)
            dve.wait_ge(*read("cum"))
            head_norm("fk", fk_t, [col("kg")])

        copy1(UNIT["fv"], fv_nat[:, 1, :], mid=fox_gates)

        def fox_probs(g, u):
            hg, qt = g // 2, g % 2
            nk = P * (qt + 1)
            cs = slice(4 * g, 4 * g + 4)
            cum_q = logf[:, 5, 8 * qt + 4 * hg:8 * qt + 4 * hg + 4].rearrange("p (c a) -> p a c", a=2)
            dve.wait_ge(*fill(("s", ("f", g), 0)))
            dve.wait_ge(*fill(("s", ("f", g), 1)))
            both = bank[:, 0:2, :].rearrange("p n (a k) -> p (n a) k", a=2)
            step(dve.tensor_reduce(peak[:, cs], both[:, :, 0:nk], AX_X, ALU.max))
            step(dve.tensor_tensor(cut(peak[:, cs], 2), cut(peak[:, cs], 2), cum_q, ALU.add))
            dve.tensor_tensor(cut(shift[:, cs], 2), cum_q, cut(peak[:, cs], 2), ALU.subtract)\
                .then_inc(*shift_ready.up(("f", g)))
            lo_half(2 * u + 4)
            e = cut(hn[:, g % 2, :], 4)
            dve.wait_ge(*read(("s", ("f", g), 0)))
            dve.wait_ge(*read(("s", ("f", g), 1)))
            recip_total(g, 4)
            for a in range(4):
                ins = dve.tensor_scalar(e[:, a, 0:nk], e[:, a, 0:nk], inv[:, 4 * g + a:4 * g + a + 1], None,
                                        ALU.mult)
                if a < 3:
                    step(ins, wait=False)
            ins.then_inc(*probs_ready.up(("f", g)))

        def fox_unit(g, u, dst):
            fox_probs(g, u)
            dve.wait_ge(half_used, 2 * u + 2)
            src = gemm[:, 2 * (u % 2) + 1, :]
            if dst is not None:
                dve.tensor_copy(dst, cut(src, 2) if len(dst.shape) == 3 else src)\
                    .then_inc(evacuated[u % 2], 1)
            lo_half(2 * u + 5)

        def rope(name, x):
            sin = sin_m.rearrange("p (a b) -> p a b", a=1).to_broadcast((P, 2, S))
            cos = cos_m.rearrange("p (a b) -> p a b", a=1).to_broadcast((P, 4, S))
            for b in range(2):
                dve.wait_ge(*fill(("rot", name, b)))
                dve.tensor_tensor(rope_tmp[:, 2 * b:2 * b + 2, :], cut(bank[:, b, :], 2), sin, ALU.mult)\
                    .then_inc(freed[b], 1)
            step(dve.tensor_tensor(x, x, cos, ALU.mult))
            dve.wait_ge(*read(("rot", name, 0)))
            dve.wait_ge(*read(("rot", name, 1)))
            dve.tensor_tensor(x, x, rope_tmp, ALU.add).then_inc(*roped.up(name))

        fox_unit(0, UNIT["rq"], rq_t[:, 2:4, :])
        fox_unit(1, UNIT["rk"], rk_t[:, 2:4, :])
        rope("q", rq_t)
        fox_unit(2, UNIT["rv"], rv_nat[:, 1, :])
        rope("k", rk_t)
        fox_unit(3, UNIT["fog"], None)
        dve.wait_ge(*set_done(UNIT["fog"]))
        step(dve.tensor_scalar(fog_t, fog_t, 1.0, None, ALU.add))
        step(dve.reciprocal(fog_t, fog_t))
        dve.wait_ge(loaded["decay"], 16)

        def decay(a):
            dve.wait_ge(*fill(("rs", a)))
            st = hn[:, a // 2, (a % 2) * NB:(a % 2) * NB + S + P]
            step(dve.tensor_tensor(st[:, 0:S], bank[:, a % 2, 0:S], decay_m[:, a, :], ALU.mult), wait=False)
            dve.tensor_tensor(st[:, S:S + P], bank[:, a % 2, S:S + P], decay_m[:, a, 0:P], ALU.mult)\
                .then_inc(freed[a % 2], 1)
            dve.wait_ge(*read(("rs", a)))
            dve.engine_nop().then_inc(*decayed.up(a))

        decay(0)
        decay(1)
        u = UNIT["rg"]
        head_inverse("fo", 16, flat(fk_t))
        lo_half(2 * u + 4)
        head_norm("fo", fq_t, [col("foxg", c) for c in range(4)], fog_t)
        split_lo("fo", (slice(None), slice(0, 4), slice(None)), fq_t)
        decay(2)
        decay(3)
        for b in range(2):
            dve.wait_ge(*((bank0_done, u + 1) if b == 0 else (half_used, 2 * u + 2)))
            dve.tensor_copy(rg_t[:, 2 * b:2 * b + 2, :], cut(gemm[:, 2 * (u % 2) + b, :], 2))\
                .then_inc(evacuated[u % 2], 1)
        dve.wait_ge(*set_done(u))
        dve.engine_nop().then_inc(*rg_kept.up(0))
        head_inverse("ro", 8)
        dve.wait_ge(*rg_exp.at(0))
        step(dve.tensor_scalar(rg_exp_t, rg_exp_t, 1.0, None, ALU.add))
        step(dve.reciprocal(rg_exp_t, rg_exp_t))
        step(dve.tensor_tensor(rg_t, rg_t, rg_exp_t, ALU.mult))
        head_norm("ro", rq_t, [col("retg", c) for c in range(4)], rg_t)
        split_lo("ro", (slice(None), slice(4, 8), slice(None)), rq_t)
        lo_half(2 * u + 5)
        dve.wait_ge(*read(("row", "gate_m", 1)))
        add_residual(UNIT["out2"], 0, gate_m_row)
        add_residual(UNIT["out2"] + 1, 1, gate_m_row, tail=False)
        dve.wait_ge(*read(("row", "scale_f", 1)))
        dve.wait_ge(*read(("row", "shift_f", 1)))
        norm("mlp2", UNIT["out2"] + 1)
        dve.wait_ge(*read(("row", "gate_f", 1)))
        mlp(2)

    @block.gpsimd
    def _(gp):
        gp.memset(eps[:, :], EPS).then_inc(set_up, 1)
        gp.memset(power[:, :], -0.5).then_inc(set_up, 1)
        gp.memset(mask_bf[:, :], 0.0).then_inc(set_up, 1)
        def load_gain(n):
            g = GAINS.index(n)
            gp.dma_start(gain, d["gains"][g:g + 1, :].to_broadcast((P, D))).then_inc(loaded["gain_" + n], 16)


        def root(n, t):
            c = squares.order.index((n, t))
            gp.wait_ge(*squares.at((n, t)))
            gp.tensor_scalar(stat[:, c:c + 1], stat[:, c:c + 1], 1.0 / D, EPS, ALU.mult, ALU.add)\
                .then_inc(*mean_done.up((n, t)))
            gp.wait_ge(*mean_done.at((n, t)))
            gp.tensor_tensor(rstd[:, c:c + 1], stat[:, c:c + 1], power[:, :], ALU.pow)\
                .then_inc(*rstd_done.up((n, t)))

        def roots(n):
            for t in range(T):
                root(n, t)

        def next_gain(last, n):
            gp.wait_ge(*normed.at((last, T - 1)))
            load_gain(n)

        roots("mix0")
        gp.wait_ge(*read("bias_row"))
        gp.dma_start(rows_dram, bias_row[0:4, :]).then_inc(bias_stored, 16)
        gp.dma_start(cols[:, :], d["cols"]).then_inc(loaded["consts"], 16)
        gp.dma_start(lam_in, d["lam"].to_broadcast((P, 4, 64))).then_inc(loaded["lam"], 16)
        gp.dma_start(ones[:, :], d["ones"]).then_inc(loaded["consts"], 16)
        for t in range(T):
            gp.dma_start(mem_rows[:, t, :], d["mem"][t * P:(t + 1) * P, :]).then_inc(loaded["mem"], 16)
        gp.dma_start(flat(pool_w), d["pool_w"]).then_inc(loaded["pool"], 16)
        gp.dma_start(work[:, 5120:7168], d["pool"]).then_inc(loaded["pool"], 16)
        gp.dma_start(ff_raw[:, :, :], d["ff"]).then_inc(loaded["ff"], 16)
        gp.wait_ge(bias_stored, 16)
        for dst, offset, n in ((flip1, 0, S), (flip0, P, P)):
            src = bass.AP(tensor=rows_dram.tensor, offset=offset, ap=[[1, P], [384, 4], [1, n]])
            gp.dma_start(dst, src).then_inc(loaded["flipped"], 16)
        gp.wait_ge(set_up, 3)
        gp.affine_select(out=mask_bf[:, :], in_=mask_bf[:, :], compare_op=ALU.is_ge, fill=NEG, base=0,
                         pattern=[[-1, P]], channel_multiplier=1).then_inc(set_up, 1)
        gp.wait_ge(loaded["ident"], 16)
        gp.tensor_copy(ident_bf[:, :], ident[:, :]).then_inc(set_up, 1)
        next_gain("mix0", "mem")
        roots("mem")
        next_gain("mem", "x0")
        gp.wait_ge(*read(("bias", 1)))
        gp.affine_select(out=bias1[:, :, P:S], in_=bias1[:, :, P:S], compare_op=ALU.is_ge, fill=NEG, base=0,
                         pattern=[[0, 4], [-1, P]], channel_multiplier=1).then_inc(*bias_masked.up(0))
        gp.wait_ge(*read(("bias", 2)))
        gp.affine_select(out=bias0, in_=bias0, compare_op=ALU.is_ge, fill=NEG, base=0,
                         pattern=[[0, 4], [-1, P]], channel_multiplier=1).then_inc(*bias_masked.up(1))
        gp.wait_ge(*read(("s", ("d", 3), 1)))
        gp.dma_start(c_act, d["c"].to_broadcast((P, D))).then_inc(loaded["c"], 16)
        roots("x0")
        next_gain("x0", "mlp0")

        def ada_loads(m):
            gp.wait_ge(*fill(("o", ("x" + str(m), 3))))
            if m == 0:
                gp.dma_start(flat(ada), d["w_ada"][0]).then_inc(ada_landed, 16)
            else:
                gp.wait_ge(ada_used, 8)
                gp.dma_start(flat(ada), d["w_ada"][8]).then_inc(ada_landed, 16)

        def more_ada(m):
            with gp.Fori(8 * m + 1, 8 * m + 8) as i:
                gp.wait_ge(ada_used, i)
                gp.dma_start(flat(ada), d["w_ada"][i]).then_inc(ada_landed, 16)

        ada_loads(0)
        roots("mlp0")
        next_gain("mlp0", "mix1")
        more_ada(0)
        roots("mix1")
        next_gain("mix1", "x1")
        roots("x1")
        next_gain("x1", "mlp1")
        ada_loads(1)
        gp.dma_start(const2, d["second"]).then_inc(loaded["const2"], 16)
        roots("mlp1")
        next_gain("mlp1", "final")
        more_ada(1)
        roots("final")
        roots("mix2")
        gp.wait_ge(*normed.at(("mix2", T - 1)))
        gp.dma_start(flat(decay_m), d["decay"]).then_inc(loaded["decay"], 16)
        roots("mlp2")


def kernel(**inputs):
    import numpy as _np
    import concourse.bacc as _bacc
    from concourse.bass_utils import run_bass_kernel_spmd as _run

    a = {k: _np.asarray(v) for k, v in inputs.items()}
    weights = {"ab_in": a["ab_w_in"][0], "conv_in": a["conv_w_in"][0], "conv_out": a["conv_w_out"][0],
               "out2": a["w_out_2"][0], "w1_2": a["w_mlp_in_2"][0], "w2_2": a["w_mlp_out_2"][0]}
    weights["ab_out"] = _np.concatenate([a["ab_w_out"][0][512:], a["ab_w_out"][0][:512]])
    for l in range(2):
        weights[f"wkv{l}"], weights[f"wq{l}"], weights[f"wo{l}"] = (
            a["xattn_wkv"][l], a["xattn_wq"][l], a["xattn_wo"][l])
        weights[f"w1_{l}"], weights[f"w2_{l}"] = a["mlp_w1"][l], a["mlp_w2"][l]
    w_in = a["w_in_2"][0]
    weights["in2"] = _np.concatenate([w_in[:, :2048], w_in[:, 2056:]], axis=1)
    stream = _np.stack([weights[n][D * r:D * (r + 1), NB * c:NB * (c + 1)] for n, r, c in UNITS])
    stream = stream.reshape(NH, HC, P, NB).transpose(0, 2, 1, 3)
    columns = [a["subln_g"][0][:, None], a["pool_scale"][0].reshape(4, P).T,
               a["conv_w"][0].reshape(24, P).T,
               _np.tile(a["q_norm_gain_2"][0], 2)[:, None], _np.tile(a["k_norm_gain_2"][0], 2)[:, None],
               a["fox_out_gain_2"][0].reshape(4, P).T, a["ret_out_gain_2"][0].T,
               a["b_ada_2"][0].reshape(48, P).T, _np.broadcast_to(a["b_forget_2"], (P, 8)),
               _np.repeat(_np.eye(2, dtype=_np.float32), 64, axis=0)]
    gains = {"mix0": a["norm_mix_g"][0], "mem": a["mem_norm_g"], "x0": a["norm_xattn_g"][0],
             "mlp0": a["norm_mlp_g"][0], "mix1": a["norm_mix_g"][1], "x1": a["norm_xattn_g"][1],
             "mlp1": a["norm_mlp_g"][1], "final": a["final_norm_g"]}
    arrays = {
        "weights": stream,
        "x": a["x"][0], "mem": a["mem"][0],
        "cols": _np.concatenate(columns, axis=1),
        "gains": _np.stack([gains[n] for n in GAINS]),
        "rel_bias": a["rel_bias"],
        "lam": _np.stack([a["lambda_q1"], a["lambda_k1"], a["lambda_q2"], a["lambda_k2"]], axis=1),
        "pool_w": a["pool_w"][0].transpose(1, 0, 2).reshape(P, -1),
        "ff": w_in[:, 2048:2056].reshape(KC, P, 8).transpose(1, 0, 2),
        "c": a["c_2"],
        "w_ada": a["w_ada_2"][0].T.reshape(ADA_LOADS, ADA_COLS, P, D).transpose(0, 2, 1, 3)
                 .reshape(ADA_LOADS, P, ADA_COLS * D),
    }
    arrays.update(constants())
    arrays = {k: _np.ascontiguousarray(v) for k, v in arrays.items()}
    nc = _bacc.Bacc("TRN2", target_bir_lowering=False, num_devices=1)
    d = {k: nc.dram_tensor("in_" + k, v.shape, mybir.dt.from_np(v.dtype), kind="ExternalInput").ap()
         for k, v in arrays.items()}
    out = nc.dram_tensor("out_y", (S, D), F32, kind="ExternalOutput").ap()
    build(nc, d, out)
    r = _run(nc, [{"in_" + k: v for k, v in arrays.items()}], core_ids=[0])
    return r.results[0]["out_y"].reshape(1, S, D)
```
